# Optimizing a Trainium2 kernel written in Bass

```python
import jax, jax.numpy as jnp
from jax import lax
import numpy as np

D_MODEL = 1024
BATCH = 1
SEQ = 1024
DEPTH = 2
DEC_BATCH = 8
DEC_SEQ = 16
PAST_LEN = 2048

CHUNK = 64
N_MIXERS = 2
N_CONV_LAYERS = (DEPTH + 1) // 2
N_HGRN_LAYERS = DEPTH // 2
CONV_K = 31
HG_HEADS = 8
HG_DK = D_MODEL // HG_HEADS
HG_DV = D_MODEL // HG_HEADS
HG_BLOCK = 16
D_FF = 2816
FFN_K = 3
EPS = 1e-6

kernel_name = 'hybrid_conformer_hgrn2_stream_step'

def rmsnorm(x, g):
    xf = x.astype(jnp.float32)
    y = xf * lax.rsqrt(jnp.mean(xf * xf, axis=-1, keepdims=True) + EPS)
    return (y * g.astype(jnp.float32)).astype(x.dtype)

def layernorm(x, g, b):
    xf = x.astype(jnp.float32)
    mu = jnp.mean(xf, axis=-1, keepdims=True)
    var = jnp.mean(jnp.square(xf - mu), axis=-1, keepdims=True)
    y = (xf - mu) * lax.rsqrt(var + EPS)
    return (y * g.astype(jnp.float32) + b.astype(jnp.float32)).astype(x.dtype)

def causal_dwconv(xp, w, b):
    c = xp.shape[-1]
    y = lax.conv_general_dilated(xp, w[:, None, :].astype(xp.dtype), (1,), 'VALID',
                                 dimension_numbers=('NWC', 'WIO', 'NWC'),
                                 feature_group_count=c)
    return y + b

def conv_module(h, buf, w_pw1, b_pw1, w_dw, b_dw, ln_g, ln_b, w_pw2, b_pw2):
    u = h @ w_pw1 + b_pw1
    a, gt = jnp.split(u, 2, axis=-1)
    glu = a * jax.nn.sigmoid(gt)
    xp = jnp.concatenate([buf.astype(glu.dtype), glu], axis=1)
    new_buf = xp[:, xp.shape[1] - (CONV_K - 1):]
    y = causal_dwconv(xp, w_dw, b_dw)
    y = jax.nn.silu(layernorm(y, ln_g, ln_b))
    return y @ w_pw2 + b_pw2, new_buf

def _to_blocks(a, pad, c):
    bsz, t, _ = a.shape
    a = jnp.pad(a, ((0, 0), (0, pad), (0, 0)))
    a = a.reshape(bsz, (t + pad) // HG_BLOCK, HG_BLOCK, HG_HEADS, c)
    return a.transpose(1, 0, 3, 2, 4)

def hgrn2_mix(h, s0, w_in, lb, norm_w, w_o):
    bsz, t, _ = h.shape
    proj = (h @ w_in).astype(jnp.float32)
    q, fl, iv, g = jnp.split(proj, 4, axis=-1)
    f = lb + (1.0 - lb) * jax.nn.sigmoid(fl)
    log_f = jnp.log(f)
    k = 1.0 - f
    pad = (-t) % HG_BLOCK
    qb = _to_blocks(q, pad, HG_DK)
    kb = _to_blocks(k, pad, HG_DK)
    ib = _to_blocks(iv, pad, HG_DV)
    lfb = _to_blocks(log_f, pad, HG_DK)
    mask = jnp.tril(jnp.ones((HG_BLOCK, HG_BLOCK), dtype=bool))

    def step(s, blk):
        qc, kc, ic, lfc = blk
        bcum = jnp.cumsum(lfc, axis=2)
        diff = bcum[:, :, :, None, :] - bcum[:, :, None, :, :]
        decay = jnp.where(mask[:, :, None], jnp.exp(jnp.minimum(diff, 0.0)), 0.0)
        scores = jnp.einsum('bhtk,bhsk,bhtsk->bhts', qc, kc, decay)
        o = (jnp.einsum('bhts,bhsv->bhtv', scores, ic)
             + jnp.einsum('bhtk,bhkv->bhtv', qc * jnp.exp(bcum), s))
        b_last = bcum[:, :, -1]
        s = (jnp.exp(b_last)[..., None] * s
             + jnp.einsum('bhsk,bhsv->bhkv', kc * jnp.exp(b_last[:, :, None] - bcum), ic))
        return s, o

    s_fin, o = lax.scan(step, s0.astype(jnp.float32), (qb, kb, ib, lfb))
    o = o.transpose(1, 0, 3, 2, 4).reshape(bsz, -1, HG_HEADS, HG_DV)[:, :t]
    o = o * lax.rsqrt(jnp.mean(o * o, axis=-1, keepdims=True) + EPS)
    o = o.reshape(bsz, t, D_MODEL) * norm_w.astype(jnp.float32) * jax.nn.silu(g)
    return o.astype(h.dtype) @ w_o, s_fin.astype(s0.dtype)

def conv_ffn(h, buf, w_up, b_up, w_dw, b_dw, w_down, b_down):
    u = h @ w_up + b_up
    xp = jnp.concatenate([buf.astype(u.dtype), u], axis=1)
    new_buf = xp[:, xp.shape[1] - (FFN_K - 1):]
    c = causal_dwconv(xp, w_dw, b_dw)
    a, v = jnp.split(c, 2, axis=-1)
    return (jax.nn.silu(a) * v) @ w_down + b_down, new_buf

def trunk(x, conv_bufs, hgrn_states, ffn_bufs, P):
    lb_p = jax.nn.softmax(P['hg_lb_logits'].astype(jnp.float32), axis=0)
    lbs = jnp.cumsum(lb_p, axis=0) - lb_p[0]
    conv_new, hgrn_new, ffn_new = [], [], []
    for i in range(DEPTH):
        j = i // N_MIXERS
        h = rmsnorm(x, P['norm_mix_w'][i])
        if i % N_MIXERS == 0:
            out, nb = conv_module(h, conv_bufs[j], P['cv_w_pw1'][j], P['cv_b_pw1'][j],
                                  P['cv_w_dw'][j], P['cv_b_dw'][j], P['cv_ln_g'][j],
                                  P['cv_ln_b'][j], P['cv_w_pw2'][j], P['cv_b_pw2'][j])
            conv_new.append(nb)
        else:
            out, ns = hgrn2_mix(h, hgrn_states[j], P['hg_w_in'][j], lbs[j],
                                P['hg_norm_w'][j], P['hg_w_o'][j])
            hgrn_new.append(ns)
        x = x + out
        h = rmsnorm(x, P['norm_ffn_w'][i])
        out, fb = conv_ffn(h, ffn_bufs[i], P['ff_w_up'][i], P['ff_b_up'][i], P['ff_w_dw'][i],
                           P['ff_b_dw'][i], P['ff_w_down'][i], P['ff_b_down'][i])
        ffn_new.append(fb)
        x = x + out
    y = rmsnorm(x, P['norm_final_w'])
    return y, jnp.stack(conv_new), jnp.stack(hgrn_new), jnp.stack(ffn_new)

def setup_inputs(seed: int = 0) -> dict:
    key = jax.random.key(seed)
    ks = iter(jax.random.split(key, 32))

    def nrm(shape, scale):
        return jax.random.normal(next(ks), shape, jnp.float32) * scale

    D, F = D_MODEL, D_FF
    NC, NH = N_CONV_LAYERS, N_HGRN_LAYERS
    return {
        'x_prompt': nrm((BATCH, SEQ, D), 1.0),
        'x_sample': nrm((DEC_BATCH, DEC_SEQ, D), 1.0),
        'cache_conv': nrm((NC, DEC_BATCH, CONV_K - 1, D), 0.5),
        'state_hgrn': nrm((NH, DEC_BATCH, HG_HEADS, HG_DK, HG_DV), 0.5),
        'cache_ffn': nrm((DEPTH, DEC_BATCH, FFN_K - 1, 2 * F), 1.0),
        'norm_mix_w': 1.0 + nrm((DEPTH, D), 0.02),
        'norm_ffn_w': 1.0 + nrm((DEPTH, D), 0.02),
        'norm_final_w': 1.0 + nrm((D,), 0.02),
        'cv_w_pw1': nrm((NC, D, 2 * D), D ** -0.5),
        'cv_b_pw1': nrm((NC, 2 * D), 0.02),
        'cv_w_dw': nrm((NC, CONV_K, D), CONV_K ** -0.5),
        'cv_b_dw': nrm((NC, D), 0.02),
        'cv_ln_g': 1.0 + nrm((NC, D), 0.02),
        'cv_ln_b': nrm((NC, D), 0.02),
        'cv_w_pw2': nrm((NC, D, D), D ** -0.5),
        'cv_b_pw2': nrm((NC, D), 0.02),
        'hg_w_in': nrm((NH, D, 4 * D), D ** -0.5),
        'hg_lb_logits': nrm((NH, D), 0.5),
        'hg_norm_w': 1.0 + nrm((NH, D), 0.02),
        'hg_w_o': nrm((NH, D, D), D ** -0.5),
        'ff_w_up': nrm((DEPTH, D, 2 * F), D ** -0.5),
        'ff_b_up': nrm((DEPTH, 2 * F), 0.02),
        'ff_w_dw': nrm((DEPTH, FFN_K, 2 * F), FFN_K ** -0.5),
        'ff_b_dw': nrm((DEPTH, 2 * F), 0.02),
        'ff_w_down': nrm((DEPTH, F, D), F ** -0.5),
        'ff_b_down': nrm((DEPTH, D), 0.02),
    }

def reference(x_prompt, x_sample, cache_conv, state_hgrn, cache_ffn,
              norm_mix_w, norm_ffn_w, norm_final_w,
              cv_w_pw1, cv_b_pw1, cv_w_dw, cv_b_dw, cv_ln_g, cv_ln_b, cv_w_pw2, cv_b_pw2,
              hg_w_in, hg_lb_logits, hg_norm_w, hg_w_o,
              ff_w_up, ff_b_up, ff_w_dw, ff_b_dw, ff_w_down, ff_b_down):
    P = dict(norm_mix_w=norm_mix_w, norm_ffn_w=norm_ffn_w, norm_final_w=norm_final_w,
             cv_w_pw1=cv_w_pw1, cv_b_pw1=cv_b_pw1, cv_w_dw=cv_w_dw, cv_b_dw=cv_b_dw,
             cv_ln_g=cv_ln_g, cv_ln_b=cv_ln_b, cv_w_pw2=cv_w_pw2, cv_b_pw2=cv_b_pw2,
             hg_w_in=hg_w_in, hg_lb_logits=hg_lb_logits, hg_norm_w=hg_norm_w, hg_w_o=hg_w_o,
             ff_w_up=ff_w_up, ff_b_up=ff_b_up, ff_w_dw=ff_w_dw, ff_b_dw=ff_b_dw,
             ff_w_down=ff_w_down, ff_b_down=ff_b_down)
    bp = x_prompt.shape[0]
    zero_conv = jnp.zeros((N_CONV_LAYERS, bp, CONV_K - 1, D_MODEL), x_prompt.dtype)
    zero_hgrn = jnp.zeros((N_HGRN_LAYERS, bp, HG_HEADS, HG_DK, HG_DV), jnp.float32)
    zero_ffn = jnp.zeros((DEPTH, bp, FFN_K - 1, 2 * D_FF), x_prompt.dtype)
    y_prompt, conv_p, hgrn_p, ffn_p = trunk(x_prompt, zero_conv, zero_hgrn, zero_ffn, P)
    y_sample, conv_s, hgrn_s, ffn_s = trunk(x_sample, cache_conv, state_hgrn, cache_ffn, P)
    return (y_prompt, y_sample, conv_p, hgrn_p, ffn_p, conv_s, hgrn_s, ffn_s)


_drawn_inputs = setup_inputs


def setup_inputs(seed=0):
    import zlib

    import numpy as np

    out = dict(_drawn_inputs(seed))
    spreads = {}
    factors = {'norm_final_w': 8.2,
     'cv_ln_g': 2.974,
     'cv_ln_b': 3.327,
     'hg_norm_w': 22.359,
     'cv_b_pw2': 2.715,
     'ff_b_dw': 3.55,
     'ff_b_down': 2.781}
    for name, (base, spread) in spreads.items():
        noise = np.random.default_rng([zlib.crc32(name.encode()), seed]).standard_normal(out[name].shape)
        drawn = base * np.exp(spread * noise) if base else spread * noise
        out[name] = __import__('jax').numpy.asarray(drawn.astype(out[name].dtype))
    for name, factor in factors.items():
        out[name] = (out[name] * factor).astype(out[name].dtype)
    return out
```

```python
from contextlib import ExitStack

import concourse.bass as bass
from concourse import mybir

ALU = mybir.AluOpType
ACT = mybir.ActivationFunctionType
F32 = mybir.dt.float32
F32R = mybir.dt.float32r
U8 = mybir.dt.uint8

P = 128
D = 1024
SEQ = 1024
NB, NS = 8, 16
T = SEQ + NB * NS
KD = D // P
CONV_K = 31
HIST = CONV_K - 1
FF = 2816
FT = FF // P
FGROUPS = FT // 2
HEADS = 8
EPS = 1e-6

NCH = 3
CW = T // NCH
LAST_PROMPT = SEQ - 2 * CW
TCH = T // P
PCH = SEQ // P

FFN_UNITS = 2 * FT + FT
FFN_TILES = 2 * FT + FGROUPS * KD
HG_UNITS, HG_TILES = 5, 26
U_PW1 = 0
U_PW2 = U_PW1 + 2 * KD
U_F0 = U_PW2 + KD
U_HG = U_F0 + FFN_UNITS
U_F1 = U_HG + HG_UNITS * HEADS
UNITS = U_F1 + FFN_UNITS
T_PW1 = 0
T_LN = T_PW1 + 2 * KD
T_PW2 = T_LN + 2
T_F0 = T_PW2 + KD
T_HG = T_F0 + FFN_TILES
T_F1 = T_HG + HG_TILES * HEADS
TILES = T_F1 + FFN_TILES
M_N0, M_F0, M_HG = 0, 3, 6
M_F1 = M_HG + 3 + HEADS
M_FIN = M_F1 + 3
P_N0, P_LN, P_F0, P_HG, P_F1 = (KD * n for n in range(5))
Q_N0, Q_F0, Q_HG, Q_F1, Q_FIN = (KD * n for n in range(5))

(C_MIX0, C_MIX1, C_FFN0, C_FFN1, C_FIN, C_BA, C_BG, C_BDW, C_LNG, C_LNB, C_BPW2, C_BD0, C_BD1,
 C_LB, C_HGN) = range(15)
NPAR = 15
FW0, FW1, FW2, FBU, FBD = range(5)

LEVELS = 8
STREAM_LEVELS = 5


class Count:

    def __init__(self, sem):
        self.sem, self.n, self.i, self.per = sem, 0, 0, 0

    def inc(self, ins):
        self.n += 1
        return ins.then_inc(self.sem, 1)

    def now(self):
        return self.n + self.i * self.per if self.per else self.n

    def enter(self, i, per):
        self.i, self.per, self.start = i, per, self.n

    def leave(self, times):
        assert self.n - self.start == self.per, (self.n - self.start, self.per)
        self.n = self.start + self.per * times
        self.i = self.per = 0


def build(nc, d_w, d_x, d_par, d_taps, d_ffp, d_fhist, d_chist, d_state, d_const, d_mask,
          o_y, o_convp, o_convs, o_hgp, o_hgs, o_ffn):
    with ExitStack() as ctx:
        def sb(name, shape, dt=F32):
            return ctx.enter_context(nc.sbuf_tensor(name, shape, dt))

        def sem(name):
            return ctx.enter_context(nc.semaphore(name))

        X = sb("X", [P, KD, T])
        XH = sb("XH", [P, KD, T], F32R)
        XL = sb("XL", [P, KD, T], F32R)
        WRAW = sb("WRAW", [P, 2, 1024])
        WH = sb("WH", [P, 2, 1024], F32R)
        WL = sb("WL", [P, 2, 1024], F32R)
        GH = sb("GH", [P, 2, T], F32R)
        GL = sb("GL", [P, 2, T], F32R)
        RSTD = sb("RSTD", [P, T])
        PAR = sb("PAR", [P, NPAR, KD])
        CONST = sb("CONST", [P, 2 * P + NB])
        IDENT = CONST[:, 0:P]
        ONES = CONST[:, P:2 * P]
        ROWM = CONST[:, 2 * P:2 * P + NB]
        SMALL = sb("SMALL", [P, 2 + 2 * KD + TCH])
        EPSC = SMALL[:, 0:1]
        LB = SMALL[:, 1:1 + KD]
        OMLB = SMALL[:, 1 + KD:1 + 2 * KD]
        R9 = SMALL[:, 1 + 2 * KD:1 + 2 * KD + TCH]
        PAD = SMALL[:, 1 + 2 * KD + TCH:]
        ARENA_F = 13056
        ARENA = sb("ARENA", [P, ARENA_F])
        at = [0]

        def cut(*shape):
            n = 1
            for s in shape:
                n *= s
            v = ARENA[:, at[0]:at[0] + n]
            at[0] += n
            assert at[0] <= ARENA_F, at[0]
            if len(shape) == 2:
                v = v.rearrange("p (a b) -> p a b", a=shape[0])
            return v

        GW = HIST + SEQ + NB * (HIST + NS)
        GLU = cut(KD, GW)
        TAPS = cut(CONV_K, KD)
        at[0] = 0
        EXT = 2 + SEQ + NB * (2 + NS)
        CE = EXT - 2
        SQ = cut(2, T)
        ACC = cut(T)
        at[0] = 0
        U = cut(2, EXT)
        C = cut(2, EXT)
        GT = cut(T)
        FHIST = cut(2 * FT, 2 * NB)
        UOUT = cut(2 * FT, 2 + 2 * NB)
        FFP = cut(2 * FT, 5)
        NEGB = cut(2 * FT)
        CB = cut(2 * FT)
        at[0] = 0
        QF = cut(T)
        KR = cut(T)
        FG = cut(T)
        TOT = cut(T)
        GATE = cut(T)
        VK = cut(TCH, P)
        VT = cut(TCH, P)
        SC = cut(TCH, P)
        ST = cut(PCH, P)
        SIN = cut(NB, P)
        VM = cut(NB, P)
        MASKW = cut(LEVELS * CW // 4)
        MASK = MASKW.bitcast(U8).rearrange("p (l c) -> p l c", l=LEVELS)
        OB, OSQ = FG, KR
        OSQT = OSQ.rearrange("p (c t) -> p c t", c=TCH)

        PS = ctx.enter_context(nc.psum_tensor("PS", [P, 2 * NCH, 512], F32))
        MB = ctx.enter_context(nc.psum_tensor("MB", [P, 2, 512], F32))

        def ps(n):
            return PS[:, (n % 2) * NCH:(n % 2 + 1) * NCH, 0:CW]

        def ps_bank(n, c):
            return PS[:, (n % 2) * NCH + c, 0:CW]

        def pieces(v):
            return v.rearrange("p (c w) -> p c w", c=NCH)

        def ps_prompt(n):
            return (PS[:, (n % 2) * NCH:(n % 2) * NCH + 2, 0:CW], ps_bank(n, 2)[:, 0:LAST_PROMPT])

        def ps_streams(n):
            return ps_bank(n, 2)[:, LAST_PROMPT:CW].rearrange("p (b s) -> p b s", b=NB)

        raw_ld = [sem("raw_ld0"), sem("raw_ld1")]
        w_hi = sem("w_hi")
        w_split = sem("w_split")
        ps_full = sem("ps_full")
        ps_free = [sem("ps_free0"), sem("ps_free1")]
        mb_full = sem("mb_full")
        mb_free = sem("mb_free")
        x_in = [sem(f"x_in{m}") for m in range(KD)]
        const_in = sem("const_in")
        hist_in = sem("hist_in")
        cache_out = sem("cache_out")
        fpar_in = sem("fpar_in")
        ffn_out = sem("ffn_out")
        state_in, state_out = sem("state_in"), sem("state_out")
        mask_in = sem("mask_in")
        outs = sem("outs")
        eps_rdy = sem("eps_rdy")
        lb_in, lb_exp = sem("lb_in"), sem("lb_exp")
        dv = sem("dv")
        av = sem("av")
        x_hi = sem("x_hi")
        x_lo = sem("x_lo")
        sq_rdy = sem("sq_rdy")
        sq_add = sem("sq_add")
        glu_sig = sem("glu_sig")
        glu_done = sem("glu_done")
        conv_done = sem("conv_done")
        yc_rdy = sem("yc_rdy")
        ysq_rdy = sem("ysq_rdy")
        ysq_used = sem("ysq_used")
        yn_rdy = sem("yn_rdy")
        tab_rdy = sem("tab_rdy")
        tap_done = sem("tap_done")
        ca_done = sem("ca_done")
        silu_done = sem("silu_done")
        g_rdy = sem("g_rdy")
        g_hi = sem("g_hi")
        g_lo = sem("g_lo")
        f_sig = sem("f_sig")
        gate_silu = sem("gate_silu")
        kq = sem("kq")
        osq_rdy = sem("osq_rdy")
        dg_rdy = sem("dg_rdy")
        y_rdy = sem("y_rdy")

        def third(k):
            return slice(k * CW, (k + 1) * CW)

        def lin(i, per, c):
            return i * per + c if per else c

        def full(eng, n, i=0, per=0):
            eng.wait_ge(ps_full, lin(i, per, n + 1))

        def emptied(eng, n, i=0, per=0):
            eng.wait_ge(ps_free[n % 2], lin(i, per // 2, n // 2 + 1))

        def unit_tile(u):
            def ffn(x, t0):
                if x == 0:
                    return t0
                j, k = divmod(x - 1, 6)
                ups = 3 if j == FGROUPS - 1 else 4
                return t0 + 1 + 12 * j + (k if k < ups else ups + 3 + 4 * (k - ups))
            if u < U_PW2:
                return T_PW1 + u
            if u < U_F0:
                return T_PW2 + u - U_PW2
            if u < U_HG:
                return ffn(u - U_F0, T_F0)
            if u < U_F1:
                h, k = divmod(u - U_HG, HG_UNITS)
                return T_HG + HG_TILES * h + (k if k < 4 else HG_TILES - 1)
            return ffn(u - U_F1, T_F1)

        block = ctx.enter_context(nc.Block())

        @block.sync
        def _(sp):
            def load(u, s):
                sp.dma_start(WRAW[:, s, :], d_w[u]).then_inc(raw_ld[s], 16)

            sp.dma_start(X[:, 0, :], d_x[0]).then_inc(x_in[0], 16)
            load(0, 0)
            for m in range(1, KD):
                sp.dma_start(X[:, m, :], d_x[m]).then_inc(x_in[m], 16)
            load(1, 1)
            with sp.Fori(1, UNITS // 2) as i:
                for s in range(2):
                    sp.wait_ge(w_split, i * 2 + (s - 1))
                    sp.dma_start(WRAW[:, s, :], d_w[bass.ds(i * 2 + s, 1), :, :].rearrange("a p c -> (a p) c")
                                 ).then_inc(raw_ld[s], 16)

        @block.gpsimd
        def _(pool):
            def split(u, i=0, per=0, used=None):
                s = u % 2
                pool.wait_ge(raw_ld[s], lin(i, 8 * per, 16 * (u // 2 + 1)))
                if used is None and u >= 2:
                    used = (unit_tile(u - 2) + 1, 0)
                if used is not None:
                    pool.wait_ge(ps_full, lin(i, used[1], used[0]))
                one = WRAW[:, s, 0:1]
                nc.gpsimd.tensor_tensor(PAD, one, one, ALU.mult)
                nc.gpsimd.tensor_copy(WH[:, s, :], WRAW[:, s, :]).then_inc(w_hi, 1)
                pool.wait_ge(w_hi, lin(i, per, u + 1))
                nc.gpsimd.tensor_tensor(WL[:, s, :], WRAW[:, s, :], WH[:, s, :].bitcast(F32),
                                        ALU.subtract).then_inc(w_split, 1)

            def squares(q0):
                for m in range(KD):
                    pool.wait_ge(sq_rdy, q0 + m + 1)
                    if m == 0:
                        nc.gpsimd.tensor_copy(ACC, SQ[:, 0, :]).then_inc(sq_add, 1)
                    else:
                        pool.wait_ge(sq_add, q0 + m)
                        nc.gpsimd.tensor_tensor(ACC, ACC, SQ[:, m % 2, :], ALU.add).then_inc(sq_add, 1)

            def loop(first, times, u, per_u, per_t):
                with pool.Fori(first, times) as i:
                    for k in range(per_u):
                        v = u + k + per_u * first
                        before = unit_tile(v - 2) + 1 - per_t * first
                        assert unit_tile(v - 2 + per_u) + 1 - per_t * (first + 1) == before
                        split(u + k, i, per_u, (before, per_t))

            def ffn(u0, q0):
                split(u0)
                squares(q0)
                split(u0 + 1)
                for u in range(u0 + 2, u0 + 7):
                    split(u)
                loop(1, FGROUPS - 1, u0 + 1, 6, 12)
                for u in range(u0 + 1 + 6 * (FGROUPS - 1), u0 + FFN_UNITS):
                    split(u)

            split(0)
            split(1)
            squares(Q_N0)
            loop(1, KD, U_PW1, 2, 2)
            for u in range(U_PW2, U_F0):
                split(u)
            ffn(U_F0, Q_F0)
            split(U_HG)
            squares(Q_HG)
            split(U_HG + 1)
            for u in range(U_HG + 2, U_HG + 2 * HG_UNITS):
                split(u)
            loop(1, HEADS // 2, U_HG, 2 * HG_UNITS, 2 * HG_TILES)
            ffn(U_F1, Q_F1)
            squares(Q_FIN)

        @block.tensor
        def _(pe):
            def free_slot(n, i=0, per=0):
                if per or n >= 2:
                    pe.wait_ge(ps_free[n % 2], lin(i, per // 2, n // 2))

            def product(n, parts, lows=None):
                last = len(parts) - 1
                for k, (wh, wl, xh, xl) in enumerate(parts):
                    if lows is not None:
                        pe.wait_ge(x_lo, lows + k + 1)
                    for q, (w, x) in enumerate(((wh, xh), (wh, xl), (wl, xh))):
                        for c in range(NCH):
                            ins = nc.tensor.matmul(ps_bank(n, c), w, x[:, third(c)],
                                                   start=(k == 0 and q == 0), stop=(k == last and q == 2))
                return ins

            def big(n, u, i=0, per_n=0, per_u=0, lows=None):
                pe.wait_ge(w_split, lin(i, per_u, u + 1))
                free_slot(n, i, per_n)
                s = u % 2
                parts = [(WH[:, s, k * P:(k + 1) * P], WL[:, s, k * P:(k + 1) * P],
                          XH[:, k, :], XL[:, k, :]) for k in range(KD)]
                product(n, parts, lows).then_inc(ps_full, 1)

            def stats(m0, q0):
                pe.wait_ge(sq_add, q0 + KD)
                for c in range(NCH):
                    if m0 + c >= 2:
                        pe.wait_ge(mb_free, m0 + c - 1)
                    nc.tensor.matmul(MB[:, (m0 + c) % 2, 0:CW], ONES, ACC[:, third(c)],
                                     start=True, stop=True).then_inc(mb_full, 1)

            def ffn(t0, u0, m0, q0, p0, g0):
                def down(n, u, j, per_n, per_u, gates, per_g):
                    pe.wait_ge(g_lo, lin(j, per_g, gates))
                    for m in range(KD):
                        v = u + m // 4
                        if m % 4 == 0:
                            pe.wait_ge(w_split, lin(j, per_u, v + 1))
                        free_slot(n + m, j, per_n)
                        a = (m % 4) * 2 * P
                        product(n + m, [(WH[:, v % 2, a + k * P:a + (k + 1) * P],
                                         WL[:, v % 2, a + k * P:a + (k + 1) * P],
                                         GH[:, k, :], GL[:, k, :]) for k in range(2)]).then_inc(ps_full, 1)

                big(t0, u0, lows=p0)
                stats(m0, q0)
                with pe.Fori(0, FGROUPS - 1) as j:
                    for k in range(4):
                        big(t0 + 1 + k, u0 + 1 + k, j, 12, 6)
                    down(t0 + 5, u0 + 5, j, 12, 6, g0 + 2, 2)
                n, u = t0 + 12 * (FGROUPS - 1), u0 + 6 * (FGROUPS - 1)
                for k in range(3):
                    big(n + 1 + k, u + 1 + k)
                down(n + 4, u + 4, 0, 0, 0, g0 + FT, 0)

            pe.wait_ge(const_in, 32)

            big(T_PW1, U_PW1, lows=P_N0)
            stats(M_N0, Q_N0)
            big(T_PW1 + 1, U_PW1 + 1)
            with pe.Fori(1, KD) as i:
                for k in range(2):
                    big(T_PW1 + k, U_PW1 + k, i, 2, 2)

            free_slot(T_LN)
            for k in range(KD):
                pe.wait_ge(conv_done, k + 1)
                for c in range(NCH):
                    ins = nc.tensor.matmul(ps_bank(T_LN, c), ONES, X[:, k, third(c)],
                                           start=(k == 0), stop=(k == KD - 1))
            ins.then_inc(ps_full, 1)
            free_slot(T_LN + 1)
            for k in range(KD):
                pe.wait_ge(ysq_rdy, k + 1)
                for c in range(NCH):
                    ins = nc.tensor.matmul(ps_bank(T_LN + 1, c), ONES, SQ[:, k % 2, third(c)],
                                           start=(k == 0), stop=(k == KD - 1))
                ins.then_inc(ysq_used if k < KD - 1 else ps_full, 1)

            for m in range(KD):
                big(T_PW2 + m, U_PW2 + m, lows=P_LN if m == 0 else None)

            ffn(T_F0, U_F0, M_F0, Q_F0, P_F0, 0)

            def head(t, u, h, i, per):
                n, v, pn, pu = t + h * HG_TILES, u + h * HG_UNITS, per * HG_TILES, per * HG_UNITS

                def big_h(k):
                    big(n + k, v + k, i, pn, pu, lows=P_HG if lows and k == 0 else None)

                lows = not per and h == 0
                big_h(0)
                if lows:
                    stats(M_HG, Q_HG)
                for k in range(1, 4):
                    big_h(k)

                def chunks(n, c):
                    return ps_bank(n, c // 3)[:, (c % 3) * P:(c % 3 + 1) * P]

                emptied(pe, n + 2, i, pn)
                free_slot(n + 4, i, pn)
                for c in range(TCH):
                    ins = nc.tensor.transpose(chunks(n + 4, c), VK[:, c, :], IDENT)
                ins.then_inc(ps_full, 1)
                for l in range(LEVELS):
                    pe.wait_ge(kq, lin(i, per * (LEVELS + 1), h * (LEVELS + 1) + l + 1))
                    free_slot(n + 5 + l, i, pn)
                    for c in range(TCH if l < STREAM_LEVELS else PCH):
                        a = slice(c * P, (c + 1) * P)
                        ins = nc.tensor.matmul(chunks(n + 5 + l, c), KR[:, a], QF[:, a], start=True, stop=True)
                    ins.then_inc(ps_full, 1)
                pe.wait_ge(kq, lin(i, per * (LEVELS + 1), (h + 1) * (LEVELS + 1)))
                free_slot(n + 13, i, pn)
                for c in range(TCH):
                    ins = nc.tensor.transpose(chunks(n + 13, c), KR[:, c * P:(c + 1) * P], IDENT)
                ins.then_inc(ps_full, 1)
                emptied(pe, n + 13, i, pn)
                free_slot(n + 14, i, pn)
                for c in range(PCH):
                    ins = nc.tensor.matmul(chunks(n + 14, c), VK[:, c, :], VT[:, c, :], start=True, stop=True)
                ins.then_inc(ps_full, 1)
                emptied(pe, n + 14, i, pn)
                free_slot(n + 15, i, pn)
                for c in range(TCH):
                    nc.tensor.matmul(chunks(n + 15, c), VT[:, c, :], SC[:, c, :], start=True, stop=c in (0, PCH))
                    if 0 < c < PCH:
                        nc.tensor.matmul(chunks(n + 15, c), ST[:, c - 1, :], QF[:, c * P:(c + 1) * P],
                                         start=False, stop=True)
                pe.wait_ge(state_in, lin(i, 16 * per, 16 * (h + 1)))
                for b in range(NB):
                    a = PCH * P + b * NS
                    ins = nc.tensor.matmul(chunks(n + 15, PCH)[:, b * NS:(b + 1) * NS], SIN[:, b, :],
                                           QF[:, a:a + NS], start=False, stop=True, skip_group_check=True)
                ins.then_inc(ps_full, 1)
                free_slot(n + 16, i, pn)
                for c, w in enumerate((3, 3, 2)):
                    ins = nc.tensor.matmul(ps_bank(n + 16, c)[:, 0:w * P], VK[:, PCH, :],
                                           VM[:, 3 * c:3 * c + w, :], start=True, stop=True)
                ins.then_inc(ps_full, 1)
                m = M_HG + 3 + h
                pe.wait_ge(osq_rdy, lin(i, per, h + 1))
                pe.wait_ge(mb_free, lin(i, per, m - 1))
                for c in range(TCH):
                    ins = nc.tensor.matmul(MB[:, m % 2, c:c + 1], OSQT[:, c, :], ONES[:, 0:1],
                                           start=True, stop=True)
                ins.then_inc(mb_full, 1)
                pe.wait_ge(dg_rdy, lin(i, per, h + 1))
                free_slot(n + 17, i, pn)
                for c in range(TCH):
                    ins = nc.tensor.matmul(chunks(n + 17, c), ONES, OSQT[:, c, :], start=True, stop=True)
                ins.then_inc(ps_full, 1)
                pe.wait_ge(w_split, lin(i, pu, v + 5))
                pe.wait_ge(g_lo, lin(i, per, FT + h + 1))
                for m in range(KD):
                    free_slot(n + 18 + m, i, pn)
                    s = (v + 4) % 2
                    product(n + 18 + m, [(WH[:, s, m * P:(m + 1) * P], WL[:, s, m * P:(m + 1) * P],
                                          GH[:, h, :], GL[:, h, :])]).then_inc(ps_full, 1)

            head(T_HG, U_HG, 0, 0, 0)
            head(T_HG, U_HG, 1, 0, 0)
            with pe.Fori(1, HEADS // 2) as i:
                for h in range(2):
                    head(T_HG, U_HG, h, i, 2)

            ffn(T_F1, U_F1, M_F1, Q_F1, P_F1, FT + HEADS)
            stats(M_FIN, Q_FIN)

        @block.scalar
        def _(act):
            A = nc.scalar.activation
            ac = Count(av)

            def split_x(q0, p0, gain, source, late=None):
                def high(m):
                    A(XH[:, m, :], X[:, m, :], ACT.Identity, scale=PAR[:, gain, m:m + 1]).then_inc(x_hi, 1)

                for m in range(KD):
                    source(m)
                    if p0 is not None and late is None:
                        high(m)
                    if q0 + m >= 2:
                        act.wait_ge(sq_add, q0 + m - 1)
                    A(SQ[:, m % 2, :], X[:, m, :], ACT.Square).then_inc(sq_rdy, 1)
                if late is not None:
                    full(act, late)
                    for m in range(KD):
                        high(m)

            def rms(m0):
                for c in range(NCH):
                    act.wait_ge(mb_full, m0 + c + 1)
                    A(RSTD[:, third(c)], MB[:, (m0 + c) % 2, 0:CW], ACT.Sqrt, bias=EPSC, scale=1.0 / D
                      ).then_inc(mb_free, 1)

            act.dma_start(PAR[:], d_par).then_inc(const_in, 16)
            act.dma_start(CONST[:], d_const).then_inc(const_in, 16)
            act.dma_start(TAPS, d_taps).then_inc(hist_in, 16)
            act.wait_ge(lb_in, 1)
            A(OMLB, LB, ACT.Exp).then_inc(lb_exp, 1)
            act.wait_ge(eps_rdy, 1)
            split_x(Q_N0, P_N0, C_MIX0, lambda m: act.wait_ge(x_in[m], 16))
            rms(M_N0)
            for c in range(KD):
                act.dma_start(GLU[:, c, HIST + SEQ:].rearrange("p (b s) -> p b s", b=NB)[:, :, 0:HIST],
                              d_chist[c]).then_inc(hist_in, 16)

            with act.Fori(0, KD) as c:
                emptied(act, T_PW1, c, 2)
                xc = X[:, bass.ds(c, 1), :].rearrange("p a t -> p (a t)")
                A(xc, xc, ACT.Sigmoid, bias=PAR[:, C_BG, bass.ds(c, 1)]).then_inc(glu_sig, 1)
                act.wait_ge(glu_done, c + 1)
                act.dma_start(o_convs[bass.ds(c, 1)].rearrange("a p b s -> (a p) b s"),
                              GLU[:, bass.ds(c, 1), HIST + SEQ:].rearrange("p a (b s) -> p (a b) s", b=NB)
                              [:, :, NS:NS + HIST]).then_inc(cache_out, 16)
            act.dma_start(o_convp, GLU[:, :, SEQ:SEQ + HIST]).then_inc(cache_out, 16)
            act.wait_ge(cache_out, 16 * (KD + 1))

            full(act, T_LN)
            A(pieces(RSTD[:]), ps(T_LN), ACT.Copy, scale=1.0 / D).then_inc(ps_free[T_LN % 2], 1)
            for k in range(KD):
                act.wait_ge(yc_rdy, k + 1)
                if k >= 2:
                    act.wait_ge(ysq_used, k - 1)
                A(SQ[:, k % 2, :], X[:, k, :], ACT.Square).then_inc(ysq_rdy, 1)
            full(act, T_LN + 1)
            A(pieces(RSTD[:]), ps(T_LN + 1), ACT.Sqrt, bias=EPSC, scale=1.0 / D
              ).then_inc(ps_free[(T_LN + 1) % 2], 1)
            for k in range(KD):
                act.wait_ge(yn_rdy, k + 1)
                ac.inc(A(X[:, k, :], X[:, k, :], ACT.Silu, bias=PAR[:, C_LNB, k:k + 1],
                         scale=PAR[:, C_LNG, k:k + 1]))
                act.wait_ge(av, ac.now())
                A(XH[:, k, :], X[:, k, :], ACT.Copy).then_inc(x_hi, 1)
            for m in range(KD):
                act.wait_ge(x_lo, P_LN + m + 1)
                act.dma_start(X[:, m, :], d_x[m]).then_inc(x_in[m], 16)

            def x_final(t):
                return lambda m: emptied(act, t - KD + m)

            def ffn(layer, t0, m0, q0, p0, gain, g0, late=None):
                x_final(t0)(0)
                act.dma_start(FHIST, d_fhist[layer]).then_inc(fpar_in, 16)
                act.dma_start(FFP, d_ffp[layer]).then_inc(fpar_in, 16)
                split_x(q0, p0, gain, x_final(t0), late)
                rms(m0)
                act.wait_ge(tab_rdy, layer + 1)

                def tap(n, slot, half, i, per_n, per_s, gates, per_g):
                    emptied(act, n, i, per_n)
                    act.wait_ge(g_rdy, lin(i, per_g, gates)) if per_g or gates else None
                    at = bass.ds(lin(i, per_s, slot), 1) if per_s else slice(slot, slot + 1)
                    A(C[:, half, 0:CE], U[:, half, 2:EXT], ACT.Identity, bias=CB[:, at],
                      scale=FFP[:, at, FW2:FW2 + 1].rearrange("p a b -> p (a b)")).then_inc(tap_done, 1)
                    bias = FFP[:, at, FBU:FBU + 1].rearrange("p a b -> p (a b)")
                    A(UOUT[:, at, 0:2].rearrange("p a b -> p (a b)"), U[:, half, SEQ:SEQ + 2], ACT.Identity, bias=bias)
                    ac.inc(A(UOUT[:, at, 2:].rearrange("p a (b s) -> p (a b) s", b=NB),
                             U[:, half, 2 + SEQ:].rearrange("p (b s) -> p b s", b=NB)[:, :, NS:NS + 2],
                             ACT.Identity, bias=bias))

                def silu(f, i, per):
                    act.wait_ge(ca_done, lin(i, per, f + 1))
                    A(C[:, 0, 0:CE], C[:, 0, 0:CE], ACT.Silu).then_inc(silu_done, 1)

                def high(f, i, per, done, per_t):
                    act.wait_ge(g_rdy, lin(i, per, f + 1))
                    act.wait_ge(ps_full, lin(i, per_t, done))
                    A(GH[:, (f - g0) % 2, :], GT, ACT.Copy).then_inc(g_hi, 1)

                f0 = layer * FT
                tap(t0, 0, 0, 0, 0, 0, g0, 0)
                silu(f0, 0, 0)

                def group(j, last):
                    if last:
                        n, s, g, f = t0 + 12 * j, 4 * j, g0 + 2 * j, f0 + 2 * j
                        j, pn, pslot, pf = 0, 0, 0, 0
                    else:
                        n, s, g, f, pn, pslot, pf = t0, 0, g0, f0, 12, 4, 2
                    tap(n + 1, s + 1, 1, j, pn, pslot, g, pf)
                    high(g, j, pf, n + 1, pn)
                    tap(n + 2, s + 2, 0, j, pn, pslot, g + 1, pf)
                    silu(f + 1, j, pf)
                    tap(n + 3, s + 3, 1, j, pn, pslot, g + 1, pf)
                    high(g + 1, j, pf, n + 1, pn)
                    if not last:
                        tap(n + 4, s + 4, 0, j, pn, pslot, g + 2, pf)
                        silu(f + 2, j, pf)

                with act.Fori(0, FGROUPS - 1) as j:
                    ac.enter(j, 4)
                    group(j, False)
                    ac.leave(FGROUPS - 1)
                group(FGROUPS - 1, True)
                act.wait_ge(av, ac.now())
                act.dma_start(o_ffn[layer], UOUT).then_inc(ffn_out, 16)

            ffn(0, T_F0, M_F0, Q_F0, P_F0, C_FFN0, 0, late=T_F0 - 1)

            split_x(Q_HG, P_HG, C_MIX1, x_final(T_HG))
            rms(M_HG)
            act.dma_start(VM, d_mask).then_inc(mask_in, 16)
            act.wait_ge(ffn_out, 16)

            def head(h, i, per):
                n, pn = T_HG + h * HG_TILES, per * HG_TILES
                act.dma_start(SIN, d_state[bass.ds(i * per + h, 1)].rearrange("a k b v -> (a k) b v")
                              ).then_inc(state_in, 16)
                emptied(act, n + 1, i, pn)
                A(FG, FG, ACT.Sigmoid).then_inc(f_sig, 1)
                emptied(act, n + 3, i, pn)
                A(GATE, GATE, ACT.Silu).then_inc(gate_silu, 1)
                for k, dst in ((4, VT), (13, VK)):
                    full(act, n + k, i, pn)
                    A(pieces(dst.rearrange("p c t -> p (c t)")), ps(n + k), ACT.Copy
                      ).then_inc(ps_free[(n + k) % 2], 1)
                full(act, n + 15, i, pn)
                A(pieces(OSQ), ps(n + 15), ACT.Square).then_inc(osq_rdy, 1)
                A(pieces(OB), ps(n + 15), ACT.Copy).then_inc(ps_free[(n + 15) % 2], 1)
                act.wait_ge(mb_full, lin(i, per, M_HG + 3 + h + 1))
                A(R9, MB[:, (M_HG + 3 + h) % 2, 0:TCH], ACT.Sqrt, bias=EPSC, scale=1.0 / P).then_inc(mb_free, 1)
                emptied(act, n + 16, i, pn)
                act.dma_start(o_hgp[bass.ds(i * per + h, 1)].rearrange("a k v -> (a k) v"), ST[:, PCH - 1, :]
                              ).then_inc(state_out, 16)
                act.dma_start(o_hgs[bass.ds(i * per + h, 1)].rearrange("a k b v -> (a k) b v"), VM
                              ).then_inc(state_out, 16)
                act.wait_ge(g_rdy, lin(i, per, FT + h + 1))
                A(GH[:, h, :], OB, ACT.Copy).then_inc(g_hi, 1)

            with act.Fori(0, HEADS // 2) as i:
                for h in range(2):
                    head(h, i, 2)
            act.wait_ge(state_out, 32 * HEADS)
            

            ffn(1, T_F1, M_F1, Q_F1, P_F1, C_FFN1, FT + HEADS)

            split_x(Q_FIN, None, None, x_final(TILES))
            rms(M_FIN)
            for m in range(KD):
                act.wait_ge(y_rdy, m + 1)
                act.dma_start(o_y[m], X[:, m, :]).then_inc(outs, 16)
            act.wait_ge(outs, 16 * KD)
            act.wait_ge(ffn_out, 32)

        @block.vector
        def _(dve):
            V = nc.vector
            dc = Count(dv)

            def mine():
                dve.wait_ge(dv, dc.now())

            V.memset(EPSC, EPS).then_inc(eps_rdy, 1)
            dve.wait_ge(const_in, 32)
            V.tensor_tensor(LB, PAR[:, C_LB, :], PAR[:, C_LB, :], ALU.subtract).then_inc(lb_in, 1)
            dve.wait_ge(lb_exp, 1)
            dc.inc(V.reciprocal(LB, OMLB))
            mine()
            dc.inc(V.tensor_tensor(OMLB, OMLB, LB, ALU.mult))
            mine()
            dc.inc(V.tensor_tensor(LB, OMLB, OMLB, ALU.subtract))
            mine()
            dc.inc(V.tensor_scalar(OMLB, LB, -1.0, 1.0, ALU.mult, ALU.add))

            def low(p0, gain, m):
                dve.wait_ge(x_hi, p0 + m + 1)
                V.scalar_tensor_tensor(out=XL[:, m, :], in0=X[:, m, :], scalar=PAR[:, gain, m:m + 1],
                                       in1=XH[:, m, :].bitcast(F32), op0=ALU.mult, op1=ALU.subtract
                                       ).then_inc(x_lo, 1)

            def rstd(m0):
                for c in range(NCH):
                    dve.wait_ge(mb_free, m0 + c + 1)
                    dc.inc(V.reciprocal(RSTD[:, third(c)], RSTD[:, third(c)]))
                mine()

            def scaled(n, dst, free=True):
                ins = V.tensor_tensor(pieces(dst), ps(n), pieces(RSTD[:]), ALU.mult)
                return ins.then_inc(ps_free[n % 2], 1) if free else ins

            def scaled_apart(n, prompt, streams):
                two, rest = ps_prompt(n)
                V.tensor_tensor(prompt[:, 0:2 * CW].rearrange("p (c w) -> p c w", c=2), two,
                                RSTD[:, 0:2 * CW].rearrange("p (c w) -> p c w", c=2), ALU.mult)
                V.tensor_tensor(prompt[:, 2 * CW:SEQ], rest, RSTD[:, 2 * CW:SEQ], ALU.mult)
                V.tensor_tensor(streams, ps_streams(n), RSTD[:, SEQ:T].rearrange("p (b s) -> p b s", b=NB),
                                ALU.mult).then_inc(ps_free[n % 2], 1)

            for m in range(KD):
                low(P_N0, C_MIX0, m)
            rstd(M_N0)
            dc.inc(V.memset(GLU[:, :, 0:HIST], 0.0))
            dve.wait_ge(hist_in, 16 * (KD + 1))

            with dve.Fori(0, KD) as c:
                dc.enter(c, 2 * CONV_K - 2)
                xc = X[:, bass.ds(c, 1), :].rearrange("p a t -> p (a t)")
                glu = GLU[:, bass.ds(c, 1), :].rearrange("p a t -> p (a t)")
                g_new = glu[:, HIST:HIST + SEQ]
                g_str = glu[:, HIST + SEQ:].rearrange("p (b s) -> p b s", b=NB)
                x_str = xc[:, SEQ:T].rearrange("p (b s) -> p b s", b=NB)
                full(dve, T_PW1, c, 2)
                scaled(T_PW1, xc)
                full(dve, T_PW1 + 1, c, 2)
                scaled_apart(T_PW1 + 1, g_new, g_str[:, :, HIST:])
                emptied(dve, T_PW1 + 1, c, 2)
                dve.wait_ge(glu_sig, c + 1)
                bias = PAR[:, C_BA, bass.ds(c, 1)]
                V.scalar_tensor_tensor(out=g_new, in0=g_new, scalar=bias, in1=xc[:, 0:SEQ],
                                       op0=ALU.add, op1=ALU.mult)
                V.scalar_tensor_tensor(out=g_str[:, :, HIST:], in0=g_str[:, :, HIST:], scalar=bias,
                                       in1=x_str, op0=ALU.add, op1=ALU.mult).then_inc(glu_done, 1)
                dve.wait_ge(glu_done, c + 1)
                for k in range(CONV_K):
                    w = TAPS[:, k, bass.ds(c, 1)]
                    for dst, src in ((xc[:, 0:SEQ], glu[:, k:k + SEQ]), (x_str, g_str[:, :, k:k + NS])):
                        if k == 0:
                            dc.inc(V.tensor_scalar(dst, src, w, PAR[:, C_BDW, bass.ds(c, 1)], ALU.mult, ALU.add))
                        else:
                            dve.wait_ge(dv, dc.now() - (0 if k == CONV_K - 1 and dst is x_str else 1))
                            ins = V.scalar_tensor_tensor(out=dst, in0=src, scalar=w, in1=dst,
                                                         op0=ALU.mult, op1=ALU.add)
                            if k < CONV_K - 1:
                                dc.inc(ins)
                ins.then_inc(conv_done, 1)
            dc.leave(KD)

            emptied(dve, T_LN)
            for k in range(KD):
                V.tensor_tensor(X[:, k, :], X[:, k, :], RSTD[:], ALU.subtract).then_inc(yc_rdy, 1)
            emptied(dve, T_LN + 1)
            dc.inc(V.reciprocal(RSTD[:], RSTD[:]))
            mine()
            for k in range(KD + 1):
                if k < KD:
                    V.tensor_tensor(X[:, k, :], X[:, k, :], RSTD[:], ALU.mult).then_inc(yn_rdy, 1)
                if k >= 1:
                    dve.wait_ge(x_hi, P_LN + k)
                    V.tensor_tensor(XL[:, k - 1, :], X[:, k - 1, :], XH[:, k - 1, :].bitcast(F32),
                                    ALU.subtract).then_inc(x_lo, 1)

            def add(n, m, bias=None, i=0, per=0):
                full(dve, n, i, per)
                if bias is None:
                    ins = V.tensor_tensor(pieces(X[:, m, :]), ps(n), pieces(X[:, m, :]), ALU.add)
                else:
                    ins = V.scalar_tensor_tensor(out=pieces(X[:, m, :]), in0=ps(n), scalar=PAR[:, bias, m:m + 1],
                                                 in1=pieces(X[:, m, :]), op0=ALU.add, op1=ALU.add)
                ins.then_inc(ps_free[n % 2], 1)

            for m in range(KD):
                dve.wait_ge(x_in[m], 32)
                add(T_PW2 + m, m, C_BPW2)
            for m in range(KD):
                low(P_F0, C_FFN0, m)

            def ffn(layer, t0, m0, g0, bias, hand_over):
                dve.wait_ge(fpar_in, 32 * (layer + 1))

                def col(k):
                    return FFP[:, :, k:k + 1].rearrange("p a b -> p (a b)")

                dc.inc(V.tensor_tensor(CB, col(FW0), col(FW1), ALU.add))
                mine()
                dc.inc(V.tensor_tensor(CB, CB, col(FW2), ALU.add))
                mine()
                dc.inc(V.tensor_tensor(CB, CB, col(FBU), ALU.mult))
                mine()
                dc.inc(V.tensor_tensor(CB, CB, col(FBD), ALU.add))
                dc.inc(V.tensor_scalar(NEGB, col(FBU), -1.0, None, ALU.mult))
                V.tensor_tensor(FHIST, FHIST, FFP[:, :, FBU:FBU + 1].broadcast_to([P, 2 * FT, 2 * NB]),
                                ALU.subtract).then_inc(tab_rdy, 1)
                rstd(m0)
                dve.wait_ge(tab_rdy, layer + 1)

                def up(n, slot, half, i, per_n, per_s, taps, per_t, done=None):
                    at = bass.ds(lin(i, per_s, slot), 1) if per_s else slice(slot, slot + 1)
                    u = U[:, half, :]
                    us = u[:, 2 + SEQ:].rearrange("p (b s) -> p b s", b=NB)
                    if last_up[half] is not None:
                        v, pv = last_up[half]
                        dve.wait_ge(av, lin(i, pv, v))
                    full(dve, n, i, per_n)
                    V.tensor_copy(u[:, 0:2], NEGB[:, at].broadcast_to([P, 2]))
                    V.tensor_copy(us[:, :, 0:2], FHIST[:, at, :].rearrange("p a (b s) -> p (a b) s", b=NB))
                    scaled_apart(n, u[:, 2:2 + SEQ], us[:, :, 2:])
                    dve.wait_ge(tap_done, lin(i, per_t, taps + 1))
                    c = C[:, half, 0:CE]

                    def tap(k):
                        return V.scalar_tensor_tensor(out=c, in0=u[:, k:k + CE], scalar=FFP[:, at, k:k + 1]
                                                      .rearrange("p a b -> p (a b)"),
                                                      in1=c, op0=ALU.mult, op1=ALU.add)
                    dc.inc(tap(FW1))
                    mine()
                    if half == 0:
                        tap(FW0).then_inc(ca_done, 1)
                    else:
                        dc.inc(tap(FW0))

                def gate(f, i, per):
                    dve.wait_ge(silu_done, lin(i, per, f - g0 + layer * FT + 1))
                    mine()
                    V.tensor_tensor(GT[:, 0:SEQ], C[:, 0, 0:SEQ], C[:, 1, 0:SEQ], ALU.mult)

                    def streams(half):
                        return C[:, half, 2 + SEQ:EXT].rearrange("p (b s) -> p b s", b=NB)[:, :, 0:NS]
                    V.tensor_tensor(GT[:, SEQ:T].rearrange("p (b s) -> p b s", b=NB), streams(0), streams(1),
                                    ALU.mult).then_inc(g_rdy, 1)
                    dve.wait_ge(g_hi, lin(i, per, f + 1))
                    V.tensor_tensor(GL[:, (f - g0) % 2, :], GT, GH[:, (f - g0) % 2, :].bitcast(F32),
                                    ALU.subtract).then_inc(g_lo, 1)

                a0 = layer * 2 * FT
                last_up = [None, None]
                up(t0, 0, 0, 0, 0, 0, a0, 0)

                def group(j, last):
                    if last:
                        n, s, g = t0 + 12 * j, 4 * j, g0 + 2 * j
                        j, pn, pslot, pg = 0, 0, 0, 0
                    else:
                        n, s, g, pn, pslot, pg = t0, 0, g0, 12, 4, 2
                    last_up[0], last_up[1] = (a0 + s + 1, pslot), None if not (s or pslot) else (a0 + s, pslot)
                    up(n + 1, s + 1, 1, j, pn, pslot, a0 + s + 1, pslot)
                    gate(g, j, pg)
                    up(n + 2, s + 2, 0, j, pn, pslot, a0 + s + 2, pslot)
                    last_up[0], last_up[1] = (a0 + s + 3, pslot), (a0 + s + 2, pslot)
                    up(n + 3, s + 3, 1, j, pn, pslot, a0 + s + 3, pslot)
                    gate(g + 1, j, pg)
                    if not last:
                        up(n + 4, s + 4, 0, j, pn, pslot, a0 + s + 4, pslot)
                        for m in range(KD):
                            add(n + 5 + m, m, None, j, pn)

                with dve.Fori(0, FGROUPS - 1) as j:
                    dc.enter(j, 6)
                    group(j, False)
                    dc.leave(FGROUPS - 1)
                group(FGROUPS - 1, True)
                for m in range(KD):
                    add(t0 + FFN_TILES - KD + m, m, bias)
                    if hand_over and m:
                        low(*hand_over, m - 1)
                if hand_over:
                    low(*hand_over, KD - 1)

            ffn(0, T_F0, M_F0, 0, C_BD0, (P_HG, C_MIX1))

            tot, at = {}, 0
            for l in range(1, LEVELS):
                tot[l] = (at, (T if l < STREAM_LEVELS else SEQ) >> l)
                at += tot[l][1]

            def blocks(l):
                if l == 0:
                    return FG.rearrange("p (b h) -> p b h", h=2)
                a, w = tot[l]
                return TOT[:, a:a + w].rearrange("p (b h) -> p b h", h=2)

            rstd(M_HG)
            dve.wait_ge(ffn_out, 16)
            dve.wait_ge(mask_in, 16)
            dc.inc(V.memset(SC, 0.0))
            for c in range(NCH):
                dc.inc(V.tensor_copy(MASK[:, :, c * P:(c + 1) * P], VM))
            mine()
            HEAD_DV = 20

            def head(h, i, per):
                n, pn = T_HG + h * HG_TILES, per * HG_TILES
                hh = bass.ds(i * per + h, 1)
                full(dve, n, i, pn)
                scaled(n, QF)
                full(dve, n + 1, i, pn)
                scaled(n + 1, FG)
                dve.wait_ge(f_sig, lin(i, per, h + 1))
                dc.inc(V.tensor_scalar(FG, FG, OMLB[:, hh], LB[:, hh], ALU.mult, ALU.add))
                mine()
                V.tensor_scalar(KR, FG, -1.0, 1.0, ALU.mult, ALU.add).then_inc(kq, 1)
                full(dve, n + 2, i, pn)
                scaled(n + 2, VK.rearrange("p c t -> p (c t)"))
                for l in range(1, LEVELS):
                    if l > 1:
                        mine()
                    b = blocks(l - 1)[:, 0:tot[l][1], :]
                    a, w = tot[l]
                    dc.inc(V.tensor_tensor(TOT[:, a:a + w], b[:, :, 0], b[:, :, 1], ALU.mult))
                full(dve, n + 3, i, pn)
                scaled(n + 3, GATE)
                emptied(dve, n + 4, i, pn)
                if per:
                    dve.wait_ge(state_out, lin(i, 32 * per, 32 * h))
                dc.inc(V.tensor_tensor(VM, VT[:, PCH:PCH + 1, :].broadcast_to([P, NB, P]),
                                       ROWM.rearrange("p (b a) -> p b a", a=1).broadcast_to([P, NB, P]), ALU.mult))
                for l in range(LEVELS):
                    full(dve, n + 5 + l, i, pn)
                    if l:
                        emptied(dve, n + 4 + l, i, pn)
                    if l == 0:
                        V.tensor_tensor(QF, QF, FG, ALU.mult).then_inc(kq, 1)
                    else:
                        w, m = (T if l < STREAM_LEVELS else SEQ), 1 << (l - 1)
                        kr = KR[:, 0:w].rearrange("p (b h m) -> p b h m", h=2, m=m)
                        qf = QF[:, 0:w].rearrange("p (b h m) -> p b h m", h=2, m=m)
                        b = blocks(l - 1)[:, 0:w >> l, :]
                        mine() if l == 1 else None
                        V.tensor_tensor(kr[:, :, 0, :], kr[:, :, 0, :],
                                        b[:, :, 1:2].broadcast_to([P, w >> l, m]), ALU.mult)
                        V.tensor_tensor(qf[:, :, 1, :], qf[:, :, 1, :],
                                        b[:, :, 0:1].broadcast_to([P, w >> l, m]), ALU.mult).then_inc(kq, 1)
                    sc = pieces(SC.rearrange("p c t -> p (c t)"))
                    mask = MASK[:, l:l + 1, :]
                    if l < STREAM_LEVELS:
                        V.copy_predicated(sc, mask.broadcast_to([P, NCH, CW]), ps(n + 5 + l)
                                          ).then_inc(ps_free[(n + 5 + l) % 2], 1)
                    else:
                        V.copy_predicated(sc[:, 0:2, :], mask.broadcast_to([P, 2, CW]), ps_prompt(n + 5 + l)[0])
                        V.copy_predicated(sc[:, 2, 0:LAST_PROMPT], MASK[:, l, 0:LAST_PROMPT],
                                          ps_prompt(n + 5 + l)[1]).then_inc(ps_free[(n + 5 + l) % 2], 1)
                full(dve, n + 14, i, pn)
                a, w = tot[LEVELS - 1]
                for c in range(PCH):
                    new = ps_bank(n + 14, c // 3)[:, (c % 3) * P:(c % 3 + 1) * P]
                    if c == 0:
                        ins = V.tensor_copy(ST[:, 0, :], new)
                    else:
                        mine()
                        ins = V.scalar_tensor_tensor(out=ST[:, c, :], in0=ST[:, c - 1, :],
                                                     scalar=TOT[:, a + c:a + c + 1], in1=new,
                                                     op0=ALU.mult, op1=ALU.add)
                    if c < PCH - 1:
                        dc.inc(ins)
                ins.then_inc(ps_free[(n + 14) % 2], 1)
                full(dve, n + 16, i, pn)
                a, w = tot[STREAM_LEVELS - 1]
                decay = TOT[:, a + w - NB:a + w].rearrange("p (b a) -> p b a", a=1)
                dc.inc(V.tensor_tensor(VM, SIN, decay.broadcast_to([P, NB, P]), ALU.mult))
                mine()
                V.tensor_tensor(VM[:, 0:6, :].rearrange("p (c b) v -> p c (b v)", c=2),
                                VM[:, 0:6, :].rearrange("p (c b) v -> p c (b v)", c=2), ps_prompt(n + 16)[0], ALU.add)
                V.tensor_tensor(VM[:, 6:8, :].rearrange("p b v -> p (b v)"),
                                VM[:, 6:8, :].rearrange("p b v -> p (b v)"), ps_prompt(n + 16)[1], ALU.add
                                ).then_inc(ps_free[(n + 16) % 2], 1)
                dve.wait_ge(mb_free, lin(i, per, M_HG + 3 + h + 1))
                dc.inc(V.reciprocal(R9, R9))
                mine()
                V.tensor_tensor(OSQT, IDENT.rearrange("p (a t) -> p a t", a=1).broadcast_to([P, TCH, P]),
                                R9.rearrange("p (c a) -> p c a", a=1).broadcast_to([P, TCH, P]), ALU.mult
                                ).then_inc(dg_rdy, 1)
                full(dve, n + 17, i, pn)
                V.tensor_tensor(pieces(OB), ps(n + 17), pieces(OB), ALU.mult).then_inc(ps_free[(n + 17) % 2], 1)
                emptied(dve, n + 17, i, pn)
                dve.wait_ge(gate_silu, lin(i, per, h + 1))
                V.scalar_tensor_tensor(out=OB, in0=OB, scalar=PAR[:, C_HGN, hh], in1=GATE,
                                       op0=ALU.mult, op1=ALU.mult).then_inc(g_rdy, 1)
                dve.wait_ge(g_hi, lin(i, per, FT + h + 1))
                V.tensor_tensor(GL[:, h, :], OB, GH[:, h, :].bitcast(F32), ALU.subtract).then_inc(g_lo, 1)
                for m in range(KD):
                    add(n + 18 + m, m, None, i, pn)

            with dve.Fori(0, HEADS // 2) as i:
                dc.enter(i, 2 * (1 + 7 + 1 + 7 + 1 + 1))
                for h in range(2):
                    head(h, i, 2)
                dc.leave(HEADS // 2)
            for m in range(KD):
                low(P_F1, C_FFN1, m)

            ffn(1, T_F1, M_F1, FT + HEADS, C_BD1, None)
            rstd(M_FIN)
            for m in range(KD):
                V.scalar_tensor_tensor(out=X[:, m, :], in0=X[:, m, :], scalar=PAR[:, C_FIN, m:m + 1],
                                       in1=RSTD[:], op0=ALU.mult, op1=ALU.mult).then_inc(y_rdy, 1)


def kernel(x_prompt, x_sample, cache_conv, state_hgrn, cache_ffn,
           norm_mix_w, norm_ffn_w, norm_final_w,
           cv_w_pw1, cv_b_pw1, cv_w_dw, cv_b_dw, cv_ln_g, cv_ln_b, cv_w_pw2, cv_b_pw2,
           hg_w_in, hg_lb_logits, hg_norm_w, hg_w_o,
           ff_w_up, ff_b_up, ff_w_dw, ff_b_dw, ff_w_down, ff_b_down):
    import numpy as np
    import concourse.bacc as bacc
    from concourse.bass_utils import run_bass_kernel_spmd as run

    def tiles(w):
        k, n = w.shape
        return w.reshape(k // P, P, n // P, P).transpose(2, 1, 0, 3)

    def units(w):
        return tiles(w).reshape(-1, P, 1024)

    def channels(v):
        return np.swapaxes(v.reshape(*v.shape[:-1], -1, P), -1, -2)

    arr = np.asarray
    pw1 = units(arr(cv_w_pw1)[0])
    stream = []
    for c in range(KD):
        stream += [pw1[KD + c], pw1[c]]
    stream += list(units(arr(cv_w_pw2)[0]))

    def ffn_units(layer):
        up = units(arr(ff_w_up)[layer])
        down = tiles(arr(ff_w_down)[layer])
        out = [up[0]]
        for j in range(FGROUPS):
            out += [up[FT + 2 * j], up[2 * j + 1], up[FT + 2 * j + 1]]
            if j < FGROUPS - 1:
                out.append(up[2 * j + 2])
            two = down[:, :, 2 * j:2 * j + 2, :]
            for half in range(2):
                out.append(two[4 * half:4 * half + 4].transpose(1, 0, 2, 3).reshape(P, 1024))
        return out

    stream += ffn_units(0)
    w_in, w_o = units(arr(hg_w_in)[0]), tiles(arr(hg_w_o)[0])
    for h in range(HEADS):
        stream += [w_in[k * HEADS + h] for k in range(4)]
        stream.append(w_o[:, :, h, :].transpose(1, 0, 2).reshape(P, 1024))
    stream += ffn_units(1)
    assert len(stream) == UNITS

    x = np.concatenate([arr(x_prompt)[0], arr(x_sample).reshape(NB * NS, D)])
    x = x.T.reshape(KD, P, T)
    vecs = [arr(norm_mix_w)[0], arr(norm_mix_w)[1], arr(norm_ffn_w)[0], arr(norm_ffn_w)[1], arr(norm_final_w),
            arr(cv_b_pw1)[0, :D], arr(cv_b_pw1)[0, D:], arr(cv_b_dw)[0], arr(cv_ln_g)[0], arr(cv_ln_b)[0],
            arr(cv_b_pw2)[0], arr(ff_b_down)[0], arr(ff_b_down)[1], arr(hg_lb_logits)[0], arr(hg_norm_w)[0]]
    par = channels(np.stack(vecs)).transpose(1, 0, 2)
    taps = channels(arr(cv_w_dw)[0]).transpose(1, 0, 2)

    order = np.arange(2 * FT).reshape(2, FT).T.reshape(-1)
    ffp = np.stack([arr(ff_w_dw)[:, 0], arr(ff_w_dw)[:, 1], arr(ff_w_dw)[:, 2], arr(ff_b_up), arr(ff_b_dw)], 1)
    ffp = channels(ffp)[..., order].transpose(0, 2, 3, 1)
    fhist = channels(arr(cache_ffn).reshape(2, NB * 2, 2 * FF))[..., order].transpose(0, 2, 3, 1)
    chist = channels(arr(cache_conv)[0]).transpose(3, 2, 0, 1)
    state = arr(state_hgrn)[0].transpose(1, 2, 0, 3)

    s, t = np.arange(P)[:, None], np.arange(P)[None, :]
    const = np.concatenate([(s == t), np.ones((P, P), bool), (s // NS == np.arange(NB)[None, :])], 1)
    masks = [s == t]
    for l in range(1, LEVELS):
        m = 1 << (l - 1)
        masks.append((s // (2 * m) == t // (2 * m)) & (s % (2 * m) < m) & (t % (2 * m) >= m))
    mask = np.stack(masks, 1)

    nc = bacc.Bacc("TRN2", target_bir_lowering=False, num_devices=1)
    arrays, args = {}, []
    ins = {"w": np.stack(stream), "x": x, "par": par, "taps": taps, "ffp": ffp, "fhist": fhist, "chist": chist,
           "state": state, "const": const.astype(np.float32), "mask": mask.astype(np.float32)}
    for name, a in ins.items():
        a = np.ascontiguousarray(a)
        arrays["in_" + name] = a
        args.append(nc.dram_tensor("in_" + name, a.shape, mybir.dt.from_np(a.dtype), kind="ExternalInput").ap())
    outs = {"y": [KD, P, T], "convp": [P, KD, HIST], "convs": [KD, P, NB, HIST], "hgp": [HEADS, P, P],
            "hgs": [HEADS, P, NB, P], "ffn": [2, P, 2 * FT, 2 + 2 * NB]}
    for name, shape in outs.items():
        args.append(nc.dram_tensor("out_" + name, shape, F32, kind="ExternalOutput").ap())
    build(nc, *args)
    r = run(nc, [arrays], core_ids=[0]).results[0]

    y = r["out_y"].reshape(D, T).T
    convp = r["out_convp"].transpose(2, 1, 0).reshape(1, 1, HIST, D)
    convs = r["out_convs"].transpose(2, 3, 0, 1).reshape(1, NB, HIST, D)
    hgp = r["out_hgp"].reshape(1, 1, HEADS, P, P)
    hgs = r["out_hgs"].transpose(2, 0, 1, 3)[None]
    back = np.argsort(order)
    f = r["out_ffn"][:, :, back, :].transpose(0, 3, 2, 1).reshape(2, 2 + 2 * NB, 2 * FF)
    return (y[:SEQ][None], y[SEQ:].reshape(NB, NS, D), convp, hgp, f[:, None, 0:2], convs, hgs,
            f[:, 2:].reshape(2, NB, 2, 2 * FF))
```

```python
from contextlib import ExitStack

import concourse.bass as bass
from concourse import mybir

ALU = mybir.AluOpType
ACT = mybir.ActivationFunctionType
F32 = mybir.dt.float32
F32R = mybir.dt.float32r
U8 = mybir.dt.uint8

P = 128
D = 1024
SEQ = 1024
NB, NS = 8, 16
T = SEQ + NB * NS
KD = D // P
CONV_K = 31
PE_TAPS = 9
HIST = CONV_K - 1
FF = 2816
FT = FF // P
FGROUPS = FT // 2
HEADS = 8
EPS = 1e-6

NCH = 3
CW = T // NCH
LAST_PROMPT = SEQ - 2 * CW
TCH = T // P
PCH = SEQ // P

FFN_UNITS = 2 * FT + FT
FFN_TILES = 2 * FT + FGROUPS * KD
HG_UNITS, HG_TILES = 5, 26
U_PW1 = 0
U_PW2 = U_PW1 + 2 * KD
U_F0 = U_PW2 + KD
U_HG = U_F0 + FFN_UNITS
U_F1 = U_HG + HG_UNITS * HEADS
UNITS = U_F1 + FFN_UNITS
T_PW1 = 0
T_LN = T_PW1 + 3 * KD
T_PW2 = T_LN + 2
T_F0 = T_PW2 + KD
T_HG = T_F0 + FFN_TILES
T_F1 = T_HG + HG_TILES * HEADS
TILES = T_F1 + FFN_TILES
M_N0, M_F0, M_HG = 0, 3, 6
M_F1 = M_HG + 3 + HEADS
M_FIN = M_F1 + 3
P_N0, P_LN, P_F0, P_HG, P_F1 = (KD * n for n in range(5))
Q_N0, Q_F0, Q_HG, Q_F1, Q_FIN = (KD * n for n in range(5))

(C_MIX0, C_MIX1, C_FFN0, C_FFN1, C_FIN, C_BA, C_BG, C_BDW, C_LNG, C_LNB, C_BPW2, C_BD0, C_BD1,
 C_LB, C_HGN) = range(15)
NPAR = 15
FW0, FW1, FW2, FBU, FBD = range(5)

LEVELS = 8
STREAM_LEVELS = 5


def pw1_tile(what, c):
    if what == "C":
        return T_PW1 + (3 + 3 * c if c < KD - 1 else 3 * KD - 1)
    return T_PW1 + (("G", "V").index(what) if c == 0 else 3 * c + (-1 if what == "G" else 1))


def hg_tiles(prev=True, following=True):
    order = ("L0 V RB L1 G L2 W0 VT L3 F L4 W1 W2 L5 W3 W4 L6 W5 W6 L7 W7 KT NS DS Q O").split()
    order = [x for x in order if (prev or x[0] not in "RW") and (following or x not in ("F", "Q"))]
    return {name: k for k, name in enumerate(order)}


HG_HEAD0 = 2 + len(hg_tiles(prev=False))


def hg_start(h):
    return T_HG + (2 if h == 0 else HG_HEAD0 + HG_TILES * (h - 1))


def hg_unit(h, what):
    if h == 0:
        return U_HG + 2 + "VGFQ".index(what)
    return U_HG + 6 + HG_UNITS * (h - 1) + "VGWFQ".index(what)


class Count:

    def __init__(self, sem):
        self.sem, self.n, self.i, self.per = sem, 0, 0, 0

    def inc(self, ins):
        self.n += 1
        return ins.then_inc(self.sem, 1)

    def now(self):
        return self.n + self.i * self.per if self.per else self.n

    def enter(self, i, per):
        self.i, self.per, self.start = i, per, self.n

    def leave(self, times):
        assert self.n - self.start == self.per, (self.n - self.start, self.per)
        self.n = self.start + self.per * times
        self.i = self.per = 0


def build(nc, d_w, d_x, d_par, d_taps, d_ffp, d_fhist, d_chist, d_state, d_const, d_mask,
          o_y, o_convp, o_convs, o_hgp, o_hgs, o_ffn):
    with ExitStack() as ctx:
        def sb(name, shape, dt=F32):
            return ctx.enter_context(nc.sbuf_tensor(name, shape, dt))

        def sem(name):
            return ctx.enter_context(nc.semaphore(name))

        X = sb("X", [P, KD, T])
        XH = sb("XH", [P, KD, T], F32R)
        XL = sb("XL", [P, KD, T], F32R)
        WRAW = sb("WRAW", [P, 2, 1024])
        WH = sb("WH", [P, 2, 1024], F32R)
        WL = sb("WL", [P, 2, 1024], F32R)
        GH = sb("GH", [P, 2, T], F32R)
        GL = sb("GL", [P, 2, T], F32R)
        RSTD = sb("RSTD", [P, T])
        PAR = sb("PAR", [P, NPAR, KD])
        CONST = sb("CONST", [P, 2 * P + NB])
        IDENT = CONST[:, 0:P]
        ONES = CONST[:, P:2 * P]
        ROWM = CONST[:, 2 * P:2 * P + NB]
        SMALL = sb("SMALL", [P, 2 + 2 * KD + TCH])
        EPSC = SMALL[:, 0:1]
        LB = SMALL[:, 1:1 + KD]
        OMLB = SMALL[:, 1 + KD:1 + 2 * KD]
        R9 = SMALL[:, 1 + 2 * KD:1 + 2 * KD + TCH]
        PAD = SMALL[:, 1 + 2 * KD + TCH:]
        ARENA_F = 13056
        ARENA = sb("ARENA", [P, ARENA_F])
        at = [0]

        def cut(*shape):
            n = 1
            for s in shape:
                n *= s
            v = ARENA[:, at[0]:at[0] + n]
            at[0] += n
            assert at[0] <= ARENA_F, at[0]
            if len(shape) == 2:
                v = v.rearrange("p (a b) -> p a b", a=shape[0])
            return v

        GW = HIST + SEQ + NB * (HIST + NS)
        GLU = cut(KD, GW)
        TAPS = cut(CONV_K, KD)
        DIAG = cut(PE_TAPS, P)
        at[0] = 0
        EXT = 2 + SEQ + NB * (2 + NS)
        CE = EXT - 2
        SQ = cut(2, T)
        ACC = cut(T)
        at[0] = 0
        U = cut(2, EXT)
        C = cut(2, EXT)
        GT = cut(T)
        FHIST = cut(2 * FT, 2 * NB)
        UOUT = cut(2 * FT, 2 + 2 * NB)
        FFP = cut(2 * FT, 5)
        NEGB = cut(2 * FT)
        CB = cut(2 * FT)
        at[0] = 0
        QF = cut(T)
        KR = cut(T)
        FG = cut(T)
        TOT = cut(T)
        GATE = cut(T)
        VK = cut(TCH, P)
        VT = cut(TCH, P)
        SC = cut(TCH, P)
        SIN = cut(NB, P)
        ST_VM = ARENA[:, at[0]:at[0] + T]
        ST = cut(PCH, P)
        VM = cut(NB, P)
        MASKW = cut(LEVELS * CW // 4)
        MASK = MASKW.bitcast(U8).rearrange("p (l c) -> p l c", l=LEVELS)
        OB = VT.rearrange("p c t -> p (c t)")
        OSQ = ST_VM
        OSQT = OSQ.rearrange("p (c t) -> p c t", c=TCH)

        PS = ctx.enter_context(nc.psum_tensor("PS", [P, 2 * NCH, 512], F32))
        MB = ctx.enter_context(nc.psum_tensor("MB", [P, 2, 512], F32))

        def ps(n):
            return PS[:, (n % 2) * NCH:(n % 2 + 1) * NCH, 0:CW]

        def ps_bank(n, c):
            return PS[:, (n % 2) * NCH + c, 0:CW]

        def pieces(v):
            return v.rearrange("p (c w) -> p c w", c=NCH)

        def ps_prompt(n):
            return (PS[:, (n % 2) * NCH:(n % 2) * NCH + 2, 0:CW], ps_bank(n, 2)[:, 0:LAST_PROMPT])

        def ps_streams(n):
            return ps_bank(n, 2)[:, LAST_PROMPT:CW].rearrange("p (b s) -> p b s", b=NB)

        raw_ld = [sem("raw_ld0"), sem("raw_ld1")]
        w_hi = sem("w_hi")
        w_split = sem("w_split")
        ps_full = sem("ps_full")
        ps_free = [sem("ps_free0"), sem("ps_free1")]
        mb_full = sem("mb_full")
        mb_free = sem("mb_free")
        x_in = [sem(f"x_in{m}") for m in range(KD)]
        const_in = sem("const_in")
        hist_in = sem("hist_in")
        cache_out = sem("cache_out")
        fpar_in = sem("fpar_in")
        ffn_out = sem("ffn_out")
        state_in, state_out = sem("state_in"), sem("state_out")
        mask_in = sem("mask_in")
        outs = sem("outs")
        eps_rdy = sem("eps_rdy")
        lb_in, lb_exp = sem("lb_in"), sem("lb_exp")
        dv = sem("dv")
        av = sem("av")
        x_hi = sem("x_hi")
        x_lo = sem("x_lo")
        sq_rdy = sem("sq_rdy")
        sq_add = sem("sq_add")
        glu_sig = sem("glu_sig")
        glu_done = sem("glu_done")
        diag_rdy = sem("diag_rdy")
        yc_rdy = sem("yc_rdy")
        ysq_rdy = sem("ysq_rdy")
        ysq_used = sem("ysq_used")
        yn_rdy = sem("yn_rdy")
        tab_rdy = sem("tab_rdy")
        tap_done = sem("tap_done")
        ca_done = sem("ca_done")
        silu_done = sem("silu_done")
        g_rdy = sem("g_rdy")
        g_hi = sem("g_hi")
        g_lo = sem("g_lo")
        f_sig = sem("f_sig")
        gate_silu = sem("gate_silu")
        vm_rdy = sem("vm_rdy")
        kq = sem("kq")
        osq_rdy = sem("osq_rdy")
        dg_rdy = sem("dg_rdy")
        y_rdy = sem("y_rdy")

        def third(k):
            return slice(k * CW, (k + 1) * CW)

        def lin(i, per, c):
            return i * per + c if per else c

        def full(eng, n, i=0, per=0):
            eng.wait_ge(ps_full, lin(i, per, n + 1))

        def emptied(eng, n, i=0, per=0):
            eng.wait_ge(ps_free[n % 2], lin(i, per // 2, n // 2 + 1))

        def unit_tile(u):
            def ffn(x, t0):
                if x == 0:
                    return t0
                j, k = divmod(x - 1, 6)
                ups = 3 if j == FGROUPS - 1 else 4
                return t0 + 1 + 12 * j + (k if k < ups else ups + 3 + 4 * (k - ups))
            if u < U_PW2:
                return pw1_tile("GV"[u % 2], u // 2)
            if u < U_F0:
                return T_PW2 + u - U_PW2
            if u < U_HG:
                return ffn(u - U_F0, T_F0)
            if u < U_F1:
                u -= U_HG
                if u < 2:
                    return T_HG + u
                if u < 6:
                    return hg_start(0) + hg_tiles(prev=False)["VGFQ"[u - 2]]
                if u == HG_UNITS * HEADS - 1:
                    return T_F1 - 1
                h, k = divmod(u - 6, HG_UNITS)
                tiles = hg_tiles(following=h + 1 < HEADS - 1)
                return hg_start(h + 1) + tiles[("V", "G", f"W{KD - 1}", "F", "Q")[k]]
            return ffn(u - U_F1, T_F1)

        block = ctx.enter_context(nc.Block())

        @block.sync
        def _(sp):
            def load(u, s):
                sp.dma_start(WRAW[:, s, :], d_w[u]).then_inc(raw_ld[s], 16)

            sp.dma_start(X[:, 0, :], d_x[0]).then_inc(x_in[0], 16)
            load(0, 0)
            for m in range(1, KD):
                sp.dma_start(X[:, m, :], d_x[m]).then_inc(x_in[m], 16)
            load(1, 1)
            with sp.Fori(1, UNITS // 2) as i:
                for s in range(2):
                    sp.wait_ge(w_split, i * 2 + (s - 1))
                    sp.dma_start(WRAW[:, s, :], d_w[bass.ds(i * 2 + s, 1), :, :].rearrange("a p c -> (a p) c")
                                 ).then_inc(raw_ld[s], 16)

        @block.gpsimd
        def _(pool):
            def split(u, i=0, per=0, used=None):
                s = u % 2
                pool.wait_ge(raw_ld[s], lin(i, 8 * per, 16 * (u // 2 + 1)))
                if used is None and u >= 2:
                    used = (unit_tile(u - 2) + 1, 0)
                if used is not None:
                    pool.wait_ge(ps_full, lin(i, used[1], used[0]))
                one = WRAW[:, s, 0:1]
                nc.gpsimd.tensor_tensor(PAD, one, one, ALU.mult)
                nc.gpsimd.tensor_copy(WH[:, s, :], WRAW[:, s, :]).then_inc(w_hi, 1)
                pool.wait_ge(w_hi, lin(i, per, u + 1))
                nc.gpsimd.tensor_tensor(WL[:, s, :], WRAW[:, s, :], WH[:, s, :].bitcast(F32),
                                        ALU.subtract).then_inc(w_split, 1)

            def squares(q0):
                for m in range(KD):
                    square(q0, m)

            def square(q0, m):
                pool.wait_ge(sq_rdy, q0 + m + 1)
                if m == 0:
                    nc.gpsimd.tensor_copy(ACC, SQ[:, 0, :]).then_inc(sq_add, 1)
                else:
                    pool.wait_ge(sq_add, q0 + m)
                    nc.gpsimd.tensor_tensor(ACC, ACC, SQ[:, m % 2, :], ALU.add).then_inc(sq_add, 1)

            def loop(first, times, u, per_u, per_t):
                with pool.Fori(first, times) as i:
                    for k in range(per_u):
                        v = u + k + per_u * first
                        before = unit_tile(v - 2) + 1 - per_t * first
                        assert unit_tile(v - 2 + per_u) + 1 - per_t * (first + 1) == before
                        split(u + k, i, per_u, (before, per_t))

            def ffn(u0):
                for u in range(u0 + 2, u0 + 7):
                    split(u)
                loop(1, FGROUPS - 1, u0 + 1, 6, 12)
                for u in range(u0 + 1 + 6 * (FGROUPS - 1), u0 + FFN_UNITS):
                    split(u)

            split(0)
            squares(Q_N0)
            split(1)
            for u in range(U_PW1 + 2, U_PW1 + 6):
                split(u)
            loop(1, (KD - 2) // 2, U_PW1 + 2, 4, 6)
            for u in range(U_PW2 - 2, U_PW2):
                split(u)
            split(U_PW2)
            split(U_PW2 + 1)
            for m in range(KD - 1):
                split(U_PW2 + 2 + m)
                square(Q_F0, m)
            square(Q_F0, KD - 1)
            split(U_F0 + 1)
            ffn(U_F0)
            split(U_HG)
            squares(Q_HG)
            split(U_HG + 1)
            for u in range(U_HG + 2, U_HG + 6 + 2 * HG_UNITS):
                split(u)
            loop(1, (HEADS - 2) // 2, U_HG + 6, 2 * HG_UNITS, 2 * HG_TILES)
            for u in range(U_F1 - 4, U_F1):
                split(u)
            split(U_F1)
            squares(Q_F1)
            split(U_F1 + 1)
            ffn(U_F1)
            squares(Q_FIN)

        @block.tensor
        def _(pe):
            def free_slot(n, i=0, per=0):
                if per or n >= 2:
                    pe.wait_ge(ps_free[n % 2], lin(i, per // 2, n // 2))

            def product(n, parts, lows=None):
                last = len(parts) - 1
                for k, (wh, wl, xh, xl) in enumerate(parts):
                    if lows is not None:
                        pe.wait_ge(x_lo, lows + k + 1)
                    for q, (w, x) in enumerate(((wh, xh), (wh, xl), (wl, xh))):
                        for c in range(NCH):
                            ins = nc.tensor.matmul(ps_bank(n, c), w, x[:, third(c)],
                                                   start=(k == 0 and q == 0), stop=(k == last and q == 2))
                return ins

            def big(n, u, i=0, per_n=0, per_u=0, lows=None):
                pe.wait_ge(w_split, lin(i, per_u, u + 1))
                free_slot(n, i, per_n)
                s = u % 2
                parts = [(WH[:, s, k * P:(k + 1) * P], WL[:, s, k * P:(k + 1) * P],
                          XH[:, k, :], XL[:, k, :]) for k in range(KD)]
                product(n, parts, lows).then_inc(ps_full, 1)

            def stats(m0, q0):
                pe.wait_ge(sq_add, q0 + KD)
                for c in range(NCH):
                    if m0 + c >= 2:
                        pe.wait_ge(mb_free, m0 + c - 1)
                    nc.tensor.matmul(MB[:, (m0 + c) % 2, 0:CW], ONES, ACC[:, third(c)],
                                     start=True, stop=True).then_inc(mb_full, 1)

            def ffn(t0, u0, m0, q0, p0, g0):
                def down(n, u, j, per_n, per_u, gates, per_g):
                    pe.wait_ge(g_lo, lin(j, per_g, gates))
                    for m in range(KD):
                        v = u + m // 4
                        if m % 4 == 0:
                            pe.wait_ge(w_split, lin(j, per_u, v + 1))
                        free_slot(n + m, j, per_n)
                        a = (m % 4) * 2 * P
                        product(n + m, [(WH[:, v % 2, a + k * P:a + (k + 1) * P],
                                         WL[:, v % 2, a + k * P:a + (k + 1) * P],
                                         GH[:, k, :], GL[:, k, :]) for k in range(2)]).then_inc(ps_full, 1)

                big(t0, u0, lows=p0)
                stats(m0, q0)
                with pe.Fori(0, FGROUPS - 1) as j:
                    for k in range(4):
                        big(t0 + 1 + k, u0 + 1 + k, j, 12, 6)
                    down(t0 + 5, u0 + 5, j, 12, 6, g0 + 2, 2)
                n, u = t0 + 12 * (FGROUPS - 1), u0 + 6 * (FGROUPS - 1)
                for k in range(3):
                    big(n + 1 + k, u + 1 + k)
                down(n + 4, u + 4, 0, 0, 0, g0 + FT, 0)

            pe.wait_ge(const_in, 32)

            big(T_PW1, U_PW1, lows=P_N0)
            stats(M_N0, Q_N0)
            big(T_PW1 + 1, U_PW1 + 1)

            def taps(c, i=0, per=0):
                n = pw1_tile("C", c)
                glu = GLU[:, bass.ds(lin(i, per, c), 1), :].rearrange("p a t -> p (a t)")
                glu_str = glu[:, HIST + SEQ:].rearrange("p (b s) -> p b s", b=NB)
                pe.wait_ge(glu_done, lin(i, per, c + 1))
                pe.wait_ge(diag_rdy, lin(i, per, c + 1))
                free_slot(n, i, 3 * per)
                two, rest = ps_prompt(n)
                for k in range(PE_TAPS):
                    diag, first, last = DIAG[:, k, :], k == 0, k == PE_TAPS - 1
                    for q in range(2):
                        nc.tensor.matmul(two[:, q, :], diag, glu[:, k + q * CW:k + (q + 1) * CW],
                                         start=first, stop=last)
                    nc.tensor.matmul(rest, diag, glu[:, k + 2 * CW:k + SEQ], start=first, stop=last)
                for k in range(PE_TAPS):
                    ins = nc.tensor.matmul(ps_streams(n), DIAG[:, k, :], glu_str[:, :, k:k + NS],
                                           start=k == 0, stop=k == PE_TAPS - 1)
                ins.then_inc(ps_full, 1)

            def convolved(c, i=0, per=0):
                big(pw1_tile("G", c + 1), U_PW1 + 2 * c + 2, i, 3 * per, 2 * per)
                taps(c, i, per)
                big(pw1_tile("V", c + 1), U_PW1 + 2 * c + 3, i, 3 * per, 2 * per)

            with pe.Fori(0, (KD - 2) // 2) as i:
                for c in range(2):
                    convolved(c, i, 2)
            convolved(KD - 2)
            taps(KD - 1)

            free_slot(T_LN)
            for k in range(KD):
                emptied(pe, pw1_tile("C", k))
                for c in range(NCH):
                    ins = nc.tensor.matmul(ps_bank(T_LN, c), ONES, X[:, k, third(c)],
                                           start=(k == 0), stop=(k == KD - 1))
            ins.then_inc(ps_full, 1)
            free_slot(T_LN + 1)
            for k in range(KD):
                pe.wait_ge(ysq_rdy, k + 1)
                for c in range(NCH):
                    ins = nc.tensor.matmul(ps_bank(T_LN + 1, c), ONES, SQ[:, k % 2, third(c)],
                                           start=(k == 0), stop=(k == KD - 1))
                ins.then_inc(ysq_used if k < KD - 1 else ps_full, 1)

            for m in range(KD):
                big(T_PW2 + m, U_PW2 + m, lows=P_LN if m == 0 else None)

            ffn(T_F0, U_F0, M_F0, Q_F0, P_F0, 0)

            def chunks(n, c):
                return ps_bank(n, c // 3)[:, (c % 3) * P:(c % 3 + 1) * P]

            def spread(n, h, i=0, per=0):
                pe.wait_ge(dg_rdy, lin(i, per, h + 1))
                free_slot(n, i, per * HG_TILES)
                for c in range(TCH):
                    ins = nc.tensor.matmul(chunks(n, c), ONES, OSQT[:, c, :], start=True, stop=True)
                ins.then_inc(ps_full, 1)

            def output(n, u, m, h, i=0, per=0):
                if m == 0:
                    pe.wait_ge(w_split, lin(i, per * HG_UNITS, u + 1))
                    pe.wait_ge(g_lo, lin(i, per, FT + h + 1))
                free_slot(n, i, per * HG_TILES)
                s = u % 2
                product(n, [(WH[:, s, m * P:(m + 1) * P], WL[:, s, m * P:(m + 1) * P],
                             GH[:, h % 2, :], GL[:, h % 2, :])]).then_inc(ps_full, 1)

            def sums(h, i=0, per=0):
                m = M_HG + 3 + h
                pe.wait_ge(osq_rdy, lin(i, per, h + 1))
                pe.wait_ge(mb_free, lin(i, per, m - 1))
                for c in range(TCH):
                    ins = nc.tensor.matmul(MB[:, m % 2, c:c + 1], OSQT[:, c, :], ONES[:, 0:1],
                                           start=True, stop=True)
                ins.then_inc(mb_full, 1)

            def block_of(h, i=0, per=0):
                prev, following = h > 0, per > 0 or h < HEADS - 1
                at = hg_tiles(prev, following)
                n0, pn, pu = hg_start(h), per * HG_TILES, per * HG_UNITS

                def proj(what):
                    big(n0 + at[what], hg_unit(h, what), i, pn, pu)

                def scores(l):
                    if l == 0 and not prev:
                        emptied(pe, n0 - 1)
                    pe.wait_ge(kq, lin(i, per * (LEVELS + 1), h * (LEVELS + 1) + l + 1))
                    n = n0 + at[f"L{l}"]
                    free_slot(n, i, pn)
                    for c in range(TCH if l < STREAM_LEVELS else PCH):
                        a = slice(c * P, (c + 1) * P)
                        ins = nc.tensor.matmul(chunks(n, c), KR[:, a], QF[:, a], start=True, stop=True)
                    ins.then_inc(ps_full, 1)

                def turn(n, src):
                    free_slot(n, i, pn)
                    for c in range(TCH):
                        ins = nc.tensor.transpose(chunks(n, c), src(c), IDENT)
                    ins.then_inc(ps_full, 1)

                def outputs(*ms):
                    for m in ms if prev else ():
                        output(n0 + at[f"W{m}"], hg_unit(h, "W"), m, h - 1, i, per)

                if prev:
                    sums(h - 1, i, per)
                scores(0)
                proj("V")
                if prev:
                    spread(n0 + at["RB"], h - 1, i, per)
                scores(1)
                proj("G")
                scores(2)
                outputs(0)
                emptied(pe, n0 + at["V"], i, pn)
                turn(n0 + at["VT"], lambda c: VK[:, c, :])
                scores(3)
                if following:
                    proj("F")
                scores(4)
                outputs(1, 2)
                scores(5)
                outputs(3, 4)
                scores(6)
                outputs(5, 6)
                scores(7)
                outputs(7)
                pe.wait_ge(kq, lin(i, per * (LEVELS + 1), (h + 1) * (LEVELS + 1)))
                turn(n0 + at["KT"], lambda c: KR[:, c * P:(c + 1) * P])
                emptied(pe, n0 + at["KT"], i, pn)
                pe.wait_ge(vm_rdy, lin(i, per, h + 1))
                n = n0 + at["NS"]
                free_slot(n, i, pn)
                for c, w in enumerate((3, 3, 2)):
                    ins = nc.tensor.matmul(ps_bank(n, c)[:, 0:w * P], VK[:, PCH, :],
                                           VM[:, 3 * c:3 * c + w, :], start=True, stop=True)
                ins.then_inc(ps_full, 1)
                n = n0 + at["DS"]
                free_slot(n, i, pn)
                for c in range(PCH):
                    ins = nc.tensor.matmul(chunks(n, c), VK[:, c, :], VT[:, c, :], start=True, stop=True)
                ins.then_inc(ps_full, 1)
                if following:
                    proj("Q")
                n = n0 + at["O"]
                emptied(pe, n0 + at["DS"], i, pn)
                free_slot(n, i, pn)
                for c in range(TCH):
                    nc.tensor.matmul(chunks(n, c), VT[:, c, :], SC[:, c, :], start=True, stop=c in (0, PCH))
                    if 0 < c < PCH:
                        nc.tensor.matmul(chunks(n, c), ST[:, c - 1, :], QF[:, c * P:(c + 1) * P],
                                         start=False, stop=True)
                pe.wait_ge(state_in, lin(i, 16 * per, 16 * (h + 1)))
                for b in range(NB):
                    a = PCH * P + b * NS
                    ins = nc.tensor.matmul(chunks(n, PCH)[:, b * NS:(b + 1) * NS], SIN[:, b, :],
                                           QF[:, a:a + NS], start=False, stop=True, skip_group_check=True)
                ins.then_inc(ps_full, 1)

            big(T_HG, U_HG, lows=P_HG)
            stats(M_HG, Q_HG)
            big(T_HG + 1, U_HG + 1)
            block_of(0)
            with pe.Fori(0, (HEADS - 2) // 2) as i:
                for h in range(1, 3):
                    block_of(h, i, 2)
            block_of(HEADS - 1)
            sums(HEADS - 1)
            spread(T_F1 - KD - 1, HEADS - 1)
            for m in range(KD):
                output(T_F1 - KD + m, U_F1 - 1, m, HEADS - 1)

            ffn(T_F1, U_F1, M_F1, Q_F1, P_F1, FT + HEADS)
            stats(M_FIN, Q_FIN)

        @block.scalar
        def _(act):
            A = nc.scalar.activation
            ac = Count(av)

            def split_x(q0, p0, gain, source, late=None):
                def high(m):
                    A(XH[:, m, :], X[:, m, :], ACT.Identity, scale=PAR[:, gain, m:m + 1]).then_inc(x_hi, 1)

                for m in range(KD):
                    source(m)
                    if p0 is not None and late is None:
                        high(m)
                    if q0 + m >= 2:
                        act.wait_ge(sq_add, q0 + m - 1)
                    A(SQ[:, m % 2, :], X[:, m, :], ACT.Square).then_inc(sq_rdy, 1)
                if late is not None:
                    full(act, late)
                    for m in range(KD):
                        high(m)

            def rms(m0):
                for c in range(NCH):
                    act.wait_ge(mb_full, m0 + c + 1)
                    A(RSTD[:, third(c)], MB[:, (m0 + c) % 2, 0:CW], ACT.Sqrt, bias=EPSC, scale=1.0 / D
                      ).then_inc(mb_free, 1)

            act.dma_start(PAR[:], d_par).then_inc(const_in, 16)
            act.dma_start(CONST[:], d_const).then_inc(const_in, 16)
            act.dma_start(TAPS, d_taps).then_inc(hist_in, 16)
            act.wait_ge(lb_in, 1)
            A(OMLB, LB, ACT.Exp).then_inc(lb_exp, 1)
            act.wait_ge(eps_rdy, 1)
            split_x(Q_N0, P_N0, C_MIX0, lambda m: act.wait_ge(x_in[m], 16))
            rms(M_N0)
            for c in range(KD):
                act.dma_start(GLU[:, c, HIST + SEQ:].rearrange("p (b s) -> p b s", b=NB)[:, :, 0:HIST],
                              d_chist[c]).then_inc(hist_in, 16)

            def diagonals(c, i=0, per=0):
                if per or c:
                    full(act, pw1_tile("C", c - 1), i, 3 * per)
                for k in range(PE_TAPS):
                    ins = A(DIAG[:, k, :], IDENT, ACT.Identity,
                            scale=TAPS[:, k, bass.ds(lin(i, per, c), 1)])
                ins.then_inc(diag_rdy, 1)

            def sigmoid(c, i=0, per=0):
                emptied(act, pw1_tile("G", c), i, 3 * per)
                cc = bass.ds(lin(i, per, c), 1)
                xc = X[:, cc, :].rearrange("p a t -> p (a t)")
                A(xc, xc, ACT.Sigmoid, bias=PAR[:, C_BG, cc]).then_inc(glu_sig, 1)

            def history(c, i=0, per=0):
                cc = bass.ds(lin(i, per, c), 1)
                act.wait_ge(glu_done, lin(i, per, c + 1))
                act.dma_start(o_convs[cc].rearrange("a p b s -> (a p) b s"),
                              GLU[:, cc, HIST + SEQ:].rearrange("p a (b s) -> p (a b) s", b=NB)
                              [:, :, NS:NS + HIST]).then_inc(cache_out, 16)

            act.wait_ge(hist_in, 16 * (KD + 1))
            sigmoid(0)
            diagonals(0)
            with act.Fori(0, (KD - 2) // 2) as i:
                for c in range(2):
                    history(c, i, 2)
                    sigmoid(c + 1, i, 2)
                    diagonals(c + 1, i, 2)
            for c in range(KD - 2, KD):
                history(c)
                if c < KD - 1:
                    sigmoid(c + 1)
                    diagonals(c + 1)
            act.dma_start(o_convp, GLU[:, :, SEQ:SEQ + HIST]).then_inc(cache_out, 16)
            act.wait_ge(cache_out, 16 * (KD + 1))

            full(act, T_LN)
            A(pieces(RSTD[:]), ps(T_LN), ACT.Copy, scale=1.0 / D).then_inc(ps_free[T_LN % 2], 1)
            for k in range(KD):
                act.wait_ge(yc_rdy, k + 1)
                if k >= 2:
                    act.wait_ge(ysq_used, k - 1)
                A(SQ[:, k % 2, :], X[:, k, :], ACT.Square).then_inc(ysq_rdy, 1)
            full(act, T_LN + 1)
            A(pieces(RSTD[:]), ps(T_LN + 1), ACT.Sqrt, bias=EPSC, scale=1.0 / D
              ).then_inc(ps_free[(T_LN + 1) % 2], 1)
            for k in range(KD):
                act.wait_ge(yn_rdy, k + 1)
                ac.inc(A(X[:, k, :], X[:, k, :], ACT.Silu, bias=PAR[:, C_LNB, k:k + 1],
                         scale=PAR[:, C_LNG, k:k + 1]))
                act.wait_ge(av, ac.now())
                A(XH[:, k, :], X[:, k, :], ACT.Copy).then_inc(x_hi, 1)
            for m in range(KD):
                act.wait_ge(x_lo, P_LN + m + 1)
                act.dma_start(X[:, m, :], d_x[m]).then_inc(x_in[m], 16)

            def x_final(t):
                return lambda m: emptied(act, t - KD + m)

            def ffn(layer, t0, m0, q0, p0, gain, g0, late=None):
                x_final(t0)(0)
                act.dma_start(FHIST, d_fhist[layer]).then_inc(fpar_in, 16)
                act.dma_start(FFP, d_ffp[layer]).then_inc(fpar_in, 16)
                split_x(q0, p0, gain, x_final(t0), late)
                rms(m0)
                act.wait_ge(tab_rdy, layer + 1)

                def tap(n, slot, half, i, per_n, per_s, gates, per_g):
                    emptied(act, n, i, per_n)
                    act.wait_ge(g_rdy, lin(i, per_g, gates)) if per_g or gates else None
                    at = bass.ds(lin(i, per_s, slot), 1) if per_s else slice(slot, slot + 1)
                    A(C[:, half, 0:CE], U[:, half, 2:EXT], ACT.Identity, bias=CB[:, at],
                      scale=FFP[:, at, FW2:FW2 + 1].rearrange("p a b -> p (a b)")).then_inc(tap_done, 1)
                    bias = FFP[:, at, FBU:FBU + 1].rearrange("p a b -> p (a b)")
                    A(UOUT[:, at, 0:2].rearrange("p a b -> p (a b)"), U[:, half, SEQ:SEQ + 2], ACT.Identity, bias=bias)
                    ac.inc(A(UOUT[:, at, 2:].rearrange("p a (b s) -> p (a b) s", b=NB),
                             U[:, half, 2 + SEQ:].rearrange("p (b s) -> p b s", b=NB)[:, :, NS:NS + 2],
                             ACT.Identity, bias=bias))

                def silu(f, i, per):
                    act.wait_ge(ca_done, lin(i, per, f + 1))
                    A(C[:, 0, 0:CE], C[:, 0, 0:CE], ACT.Silu).then_inc(silu_done, 1)

                def high(f, i, per, done, per_t):
                    act.wait_ge(g_rdy, lin(i, per, f + 1))
                    act.wait_ge(ps_full, lin(i, per_t, done))
                    A(GH[:, (f - g0) % 2, :], GT, ACT.Copy).then_inc(g_hi, 1)

                f0 = layer * FT
                tap(t0, 0, 0, 0, 0, 0, g0, 0)
                silu(f0, 0, 0)

                def group(j, last):
                    if last:
                        n, s, g, f = t0 + 12 * j, 4 * j, g0 + 2 * j, f0 + 2 * j
                        j, pn, pslot, pf = 0, 0, 0, 0
                    else:
                        n, s, g, f, pn, pslot, pf = t0, 0, g0, f0, 12, 4, 2
                    tap(n + 1, s + 1, 1, j, pn, pslot, g, pf)
                    high(g, j, pf, n + 1, pn)
                    tap(n + 2, s + 2, 0, j, pn, pslot, g + 1, pf)
                    silu(f + 1, j, pf)
                    tap(n + 3, s + 3, 1, j, pn, pslot, g + 1, pf)
                    high(g + 1, j, pf, n + 1, pn)
                    if not last:
                        tap(n + 4, s + 4, 0, j, pn, pslot, g + 2, pf)
                        silu(f + 2, j, pf)

                with act.Fori(0, FGROUPS - 1) as j:
                    ac.enter(j, 4)
                    group(j, False)
                    ac.leave(FGROUPS - 1)
                group(FGROUPS - 1, True)
                act.wait_ge(av, ac.now())
                act.dma_start(o_ffn[layer], UOUT).then_inc(ffn_out, 16)

            ffn(0, T_F0, M_F0, Q_F0, P_F0, C_FFN0, 0, late=T_F0 - 1)

            split_x(Q_HG, P_HG, C_MIX1, x_final(T_HG))
            rms(M_HG)
            act.dma_start(VM, d_mask).then_inc(mask_in, 16)
            act.wait_ge(ffn_out, 16)

            def load_state(h, i=0, per=0):
                act.dma_start(SIN, d_state[bass.ds(lin(i, per, h), 1)].rearrange("a k b v -> (a k) b v")
                              ).then_inc(state_in, 16)

            def root(h, i=0, per=0):
                act.wait_ge(mb_full, lin(i, per, M_HG + 3 + h + 1))
                A(R9, MB[:, (M_HG + 3 + h) % 2, 0:TCH], ACT.Sqrt, bias=EPSC, scale=1.0 / P).then_inc(mb_free, 1)

            def out_high(h, i=0, per=0):
                act.wait_ge(g_rdy, lin(i, per, FT + h + 1))
                A(GH[:, h % 2, :], OB, ACT.Copy).then_inc(g_hi, 1)

            def block_of(h, i=0, per=0):
                prev, following = h > 0, per > 0 or h < HEADS - 1
                at, n0, pn = hg_tiles(prev, following), hg_start(h), per * HG_TILES

                def tokens(what, dst):
                    full(act, n0 + at[what], i, pn)
                    A(pieces(dst.rearrange("p c t -> p (c t)")), ps(n0 + at[what]), ACT.Copy
                      ).then_inc(ps_free[(n0 + at[what]) % 2], 1)

                if prev:
                    root(h - 1, i, per)
                    out_high(h - 1, i, per)
                emptied(act, n0 + at["G"], i, pn)
                A(GATE, GATE, ACT.Silu).then_inc(gate_silu, 1)
                tokens("VT", VT)
                if following:
                    emptied(act, n0 + at["F"], i, pn)
                    A(FG, FG, ACT.Sigmoid).then_inc(f_sig, 1)
                tokens("KT", VK)
                emptied(act, n0 + at["NS"], i, pn)
                act.dma_start(o_hgs[bass.ds(lin(i, per, h), 1)].rearrange("a k b v -> (a k) b v"), VM
                              ).then_inc(state_out, 16)
                emptied(act, n0 + at["DS"], i, pn)
                act.dma_start(o_hgp[bass.ds(lin(i, per, h), 1)].rearrange("a k v -> (a k) v"), ST[:, PCH - 1, :]
                              ).then_inc(state_out, 16)
                n = n0 + at["O"]
                full(act, n, i, pn)
                act.wait_ge(state_out, lin(i, 32 * per, 32 * (h + 1)))
                A(pieces(OSQ), ps(n), ACT.Square).then_inc(osq_rdy, 1)
                A(pieces(OB), ps(n), ACT.Copy).then_inc(ps_free[n % 2], 1)
                if following:
                    load_state(h + 1, i, per)

            load_state(0)
            emptied(act, T_HG)
            A(FG, FG, ACT.Sigmoid).then_inc(f_sig, 1)
            block_of(0)
            with act.Fori(0, (HEADS - 2) // 2) as i:
                for h in range(1, 3):
                    block_of(h, i, 2)
            block_of(HEADS - 1)
            root(HEADS - 1)
            out_high(HEADS - 1)
            act.wait_ge(state_out, 32 * HEADS)

            ffn(1, T_F1, M_F1, Q_F1, P_F1, C_FFN1, FT + HEADS)

            split_x(Q_FIN, None, None, x_final(TILES))
            rms(M_FIN)
            for m in range(KD):
                act.wait_ge(y_rdy, m + 1)
                act.dma_start(o_y[m], X[:, m, :]).then_inc(outs, 16)
            act.wait_ge(outs, 16 * KD)
            act.wait_ge(ffn_out, 32)

        @block.vector
        def _(dve):
            V = nc.vector
            dc = Count(dv)

            def mine():
                dve.wait_ge(dv, dc.now())

            V.memset(EPSC, EPS).then_inc(eps_rdy, 1)
            dve.wait_ge(const_in, 32)
            V.tensor_tensor(LB, PAR[:, C_LB, :], PAR[:, C_LB, :], ALU.subtract).then_inc(lb_in, 1)
            dve.wait_ge(lb_exp, 1)
            dc.inc(V.reciprocal(LB, OMLB))
            mine()
            dc.inc(V.tensor_tensor(OMLB, OMLB, LB, ALU.mult))
            mine()
            dc.inc(V.tensor_tensor(LB, OMLB, OMLB, ALU.subtract))
            mine()
            dc.inc(V.tensor_scalar(OMLB, LB, -1.0, 1.0, ALU.mult, ALU.add))

            def low(p0, gain, m):
                dve.wait_ge(x_hi, p0 + m + 1)
                V.scalar_tensor_tensor(out=XL[:, m, :], in0=X[:, m, :], scalar=PAR[:, gain, m:m + 1],
                                       in1=XH[:, m, :].bitcast(F32), op0=ALU.mult, op1=ALU.subtract
                                       ).then_inc(x_lo, 1)

            def rstd(m0):
                for c in range(NCH):
                    dve.wait_ge(mb_free, m0 + c + 1)
                    dc.inc(V.reciprocal(RSTD[:, third(c)], RSTD[:, third(c)]))
                mine()

            def scaled(n, dst, free=True):
                ins = V.tensor_tensor(pieces(dst), ps(n), pieces(RSTD[:]), ALU.mult)
                return ins.then_inc(ps_free[n % 2], 1) if free else ins

            def scaled_apart(n, prompt, streams):
                two, rest = ps_prompt(n)
                V.tensor_tensor(prompt[:, 0:2 * CW].rearrange("p (c w) -> p c w", c=2), two,
                                RSTD[:, 0:2 * CW].rearrange("p (c w) -> p c w", c=2), ALU.mult)
                V.tensor_tensor(prompt[:, 2 * CW:SEQ], rest, RSTD[:, 2 * CW:SEQ], ALU.mult)
                V.tensor_tensor(streams, ps_streams(n), RSTD[:, SEQ:T].rearrange("p (b s) -> p b s", b=NB),
                                ALU.mult).then_inc(ps_free[n % 2], 1)

            for m in range(KD):
                low(P_N0, C_MIX0, m)
            rstd(M_N0)
            dc.inc(V.memset(GLU[:, :, 0:HIST], 0.0))
            dve.wait_ge(hist_in, 16 * (KD + 1))

            def glu_parts(c, i, per):
                cc = bass.ds(lin(i, per, c), 1)
                xc = X[:, cc, :].rearrange("p a t -> p (a t)")
                glu = GLU[:, cc, :].rearrange("p a t -> p (a t)")
                return (cc, xc, xc[:, SEQ:T].rearrange("p (b s) -> p b s", b=NB), glu,
                        glu[:, HIST + SEQ:].rearrange("p (b s) -> p b s", b=NB))

            def gate_in(c, i=0, per=0):
                n = pw1_tile("G", c)
                full(dve, n, i, 3 * per)
                scaled(n, glu_parts(c, i, per)[1])

            def glu_of(c, i=0, per=0):
                cc, xc, x_str, glu, g_str = glu_parts(c, i, per)
                g_new, n = glu[:, HIST:HIST + SEQ], pw1_tile("V", c)
                full(dve, n, i, 3 * per)
                scaled_apart(n, g_new, g_str[:, :, HIST:])
                emptied(dve, n, i, 3 * per)
                dve.wait_ge(glu_sig, lin(i, per, c + 1))
                bias = PAR[:, C_BA, cc]
                V.scalar_tensor_tensor(out=g_new, in0=g_new, scalar=bias, in1=xc[:, 0:SEQ],
                                       op0=ALU.add, op1=ALU.mult)
                V.scalar_tensor_tensor(out=g_str[:, :, HIST:], in0=g_str[:, :, HIST:], scalar=bias,
                                       in1=x_str, op0=ALU.add, op1=ALU.mult).then_inc(glu_done, 1)

            def convolve(c, i=0, per=0):
                cc, xc, x_str, glu, g_str = glu_parts(c, i, per)
                dve.wait_ge(glu_done, lin(i, per, c + 1))
                for k in range(PE_TAPS, CONV_K):
                    w = TAPS[:, k, cc]
                    if k == PE_TAPS + 8 and (per or c < KD - 1):
                        gate_in(c + 1, i, per)
                    for dst, src in ((xc[:, 0:SEQ], glu[:, k:k + SEQ]), (x_str, g_str[:, :, k:k + NS])):
                        if k == PE_TAPS:
                            dc.inc(V.tensor_scalar(dst, src, w, PAR[:, C_BDW, cc], ALU.mult, ALU.add))
                        else:
                            dve.wait_ge(dv, dc.now() - 1)
                            dc.inc(V.scalar_tensor_tensor(out=dst, in0=src, scalar=w, in1=dst,
                                                          op0=ALU.mult, op1=ALU.add))
                n = pw1_tile("C", c)
                full(dve, n, i, 3 * per)
                mine()
                V.tensor_tensor(pieces(xc), ps(n), pieces(xc), ALU.add).then_inc(ps_free[n % 2], 1)

            gate_in(0)
            glu_of(0)
            with dve.Fori(0, (KD - 2) // 2) as i:
                dc.enter(i, 2 * 2 * (CONV_K - PE_TAPS))
                for c in range(2):
                    convolve(c, i, 2)
                    glu_of(c + 1, i, 2)
                dc.leave((KD - 2) // 2)
            convolve(KD - 2)
            glu_of(KD - 1)
            convolve(KD - 1)

            emptied(dve, T_LN)
            for k in range(KD):
                V.tensor_tensor(X[:, k, :], X[:, k, :], RSTD[:], ALU.subtract).then_inc(yc_rdy, 1)
            emptied(dve, T_LN + 1)
            dc.inc(V.reciprocal(RSTD[:], RSTD[:]))
            mine()
            for k in range(KD + 1):
                if k < KD:
                    V.tensor_tensor(X[:, k, :], X[:, k, :], RSTD[:], ALU.mult).then_inc(yn_rdy, 1)
                if k >= 1:
                    dve.wait_ge(x_hi, P_LN + k)
                    V.tensor_tensor(XL[:, k - 1, :], X[:, k - 1, :], XH[:, k - 1, :].bitcast(F32),
                                    ALU.subtract).then_inc(x_lo, 1)

            def add(n, m, bias=None, i=0, per=0):
                full(dve, n, i, per)
                if bias is None:
                    ins = V.tensor_tensor(pieces(X[:, m, :]), ps(n), pieces(X[:, m, :]), ALU.add)
                else:
                    ins = V.scalar_tensor_tensor(out=pieces(X[:, m, :]), in0=ps(n), scalar=PAR[:, bias, m:m + 1],
                                                 in1=pieces(X[:, m, :]), op0=ALU.add, op1=ALU.add)
                ins.then_inc(ps_free[n % 2], 1)

            for m in range(KD):
                dve.wait_ge(x_in[m], 32)
                add(T_PW2 + m, m, C_BPW2)
            for m in range(KD):
                low(P_F0, C_FFN0, m)

            def ffn(layer, t0, m0, g0, bias, hand_over):
                dve.wait_ge(fpar_in, 32 * (layer + 1))

                def col(k):
                    return FFP[:, :, k:k + 1].rearrange("p a b -> p (a b)")

                dc.inc(V.tensor_tensor(CB, col(FW0), col(FW1), ALU.add))
                mine()
                dc.inc(V.tensor_tensor(CB, CB, col(FW2), ALU.add))
                mine()
                dc.inc(V.tensor_tensor(CB, CB, col(FBU), ALU.mult))
                mine()
                dc.inc(V.tensor_tensor(CB, CB, col(FBD), ALU.add))
                dc.inc(V.tensor_scalar(NEGB, col(FBU), -1.0, None, ALU.mult))
                V.tensor_tensor(FHIST, FHIST, FFP[:, :, FBU:FBU + 1].broadcast_to([P, 2 * FT, 2 * NB]),
                                ALU.subtract).then_inc(tab_rdy, 1)
                rstd(m0)
                dve.wait_ge(tab_rdy, layer + 1)

                def up(n, slot, half, i, per_n, per_s, taps, per_t, between=(None, None)):
                    at = bass.ds(lin(i, per_s, slot), 1) if per_s else slice(slot, slot + 1)
                    u = U[:, half, :]
                    us = u[:, 2 + SEQ:].rearrange("p (b s) -> p b s", b=NB)
                    if last_up[half] is not None:
                        v, pv = last_up[half]
                        dve.wait_ge(av, lin(i, pv, v))
                    full(dve, n, i, per_n)
                    V.tensor_copy(u[:, 0:2], NEGB[:, at].broadcast_to([P, 2]))
                    V.tensor_copy(us[:, :, 0:2], FHIST[:, at, :].rearrange("p a (b s) -> p (a b) s", b=NB))
                    scaled_apart(n, u[:, 2:2 + SEQ], us[:, :, 2:])
                    if between[0]:
                        between[0]()
                    dve.wait_ge(tap_done, lin(i, per_t, taps + 1))
                    c = C[:, half, 0:CE]

                    def tap(k):
                        return V.scalar_tensor_tensor(out=c, in0=u[:, k:k + CE], scalar=FFP[:, at, k:k + 1]
                                                      .rearrange("p a b -> p (a b)"),
                                                      in1=c, op0=ALU.mult, op1=ALU.add)
                    dc.inc(tap(FW1))
                    if between[1]:
                        between[1]()
                    mine()
                    if half == 0:
                        tap(FW0).then_inc(ca_done, 1)
                    else:
                        dc.inc(tap(FW0))

                def gate(f, i, per):
                    dve.wait_ge(silu_done, lin(i, per, f - g0 + layer * FT + 1))
                    mine()
                    V.tensor_tensor(GT[:, 0:SEQ], C[:, 0, 0:SEQ], C[:, 1, 0:SEQ], ALU.mult)

                    def streams(half):
                        return C[:, half, 2 + SEQ:EXT].rearrange("p (b s) -> p b s", b=NB)[:, :, 0:NS]
                    V.tensor_tensor(GT[:, SEQ:T].rearrange("p (b s) -> p b s", b=NB), streams(0), streams(1),
                                    ALU.mult).then_inc(g_rdy, 1)
                    dve.wait_ge(g_hi, lin(i, per, f + 1))
                    V.tensor_tensor(GL[:, (f - g0) % 2, :], GT, GH[:, (f - g0) % 2, :].bitcast(F32),
                                    ALU.subtract).then_inc(g_lo, 1)

                a0 = layer * 2 * FT
                last_up = [None, None]
                up(t0, 0, 0, 0, 0, 0, a0, 0)

                def group(j, last):
                    if last:
                        n, s, g = t0 + 12 * j, 4 * j, g0 + 2 * j
                        j, pn, pslot, pg = 0, 0, 0, 0
                    else:
                        n, s, g, pn, pslot, pg = t0, 0, g0, 12, 4, 2
                    last_up[0], last_up[1] = (a0 + s + 1, pslot), None if not (s or pslot) else (a0 + s, pslot)
                    up(n + 1, s + 1, 1, j, pn, pslot, a0 + s + 1, pslot)
                    gate(g, j, pg)
                    up(n + 2, s + 2, 0, j, pn, pslot, a0 + s + 2, pslot)
                    last_up[0], last_up[1] = (a0 + s + 3, pslot), (a0 + s + 2, pslot)
                    up(n + 3, s + 3, 1, j, pn, pslot, a0 + s + 3, pslot)
                    gate(g + 1, j, pg)
                    if not last:
                        up(n + 4, s + 4, 0, j, pn, pslot, a0 + s + 4, pslot,
                           [lambda m=m: add(n + 5 + m, m, None, j, pn) for m in range(2)])
                        for m in range(2, KD):
                            add(n + 5 + m, m, None, j, pn)

                with dve.Fori(0, FGROUPS - 1) as j:
                    dc.enter(j, 6)
                    group(j, False)
                    dc.leave(FGROUPS - 1)
                group(FGROUPS - 1, True)
                for m in range(KD):
                    add(t0 + FFN_TILES - KD + m, m, bias)
                    if hand_over and m:
                        low(*hand_over, m - 1)
                if hand_over:
                    low(*hand_over, KD - 1)

            ffn(0, T_F0, M_F0, 0, C_BD0, (P_HG, C_MIX1))

            tot, at = {}, 0
            for l in range(1, LEVELS):
                tot[l] = (at, (T if l < STREAM_LEVELS else SEQ) >> l)
                at += tot[l][1]

            def blocks(l):
                if l == 0:
                    return FG.rearrange("p (b h) -> p b h", h=2)
                a, w = tot[l]
                return TOT[:, a:a + w].rearrange("p (b h) -> p b h", h=2)

            rstd(M_HG)
            dve.wait_ge(ffn_out, 16)
            dve.wait_ge(mask_in, 16)
            dc.inc(V.memset(SC, 0.0))
            for c in range(NCH):
                dc.inc(V.tensor_copy(MASK[:, :, c * P:(c + 1) * P], VM))
            mine()

            def forget(h, i=0, per=0):
                hh = bass.ds(lin(i, per, h), 1)
                dve.wait_ge(f_sig, lin(i, per, h + 1))
                dc.inc(V.tensor_scalar(FG, FG, OMLB[:, hh], LB[:, hh], ALU.mult, ALU.add))

            def key():
                mine()
                V.tensor_scalar(KR, FG, -1.0, 1.0, ALU.mult, ALU.add).then_inc(kq, 1)

            def diagonals(h, i=0, per=0):
                dve.wait_ge(mb_free, lin(i, per, M_HG + 3 + h + 1))
                dc.inc(V.reciprocal(R9, R9))
                mine()
                V.tensor_tensor(OSQT, IDENT.rearrange("p (a t) -> p a t", a=1).broadcast_to([P, TCH, P]),
                                R9.rearrange("p (c a) -> p c a", a=1).broadcast_to([P, TCH, P]), ALU.mult
                                ).then_inc(dg_rdy, 1)

            def gated(n, h, i=0, per=0):
                full(dve, n, i, per * HG_TILES)
                V.tensor_tensor(pieces(OB), ps(n), pieces(OB), ALU.mult).then_inc(ps_free[n % 2], 1)
                emptied(dve, n, i, per * HG_TILES)
                dve.wait_ge(gate_silu, lin(i, per, h + 1))
                V.scalar_tensor_tensor(out=OB, in0=OB, scalar=PAR[:, C_HGN, bass.ds(lin(i, per, h), 1)], in1=GATE,
                                       op0=ALU.mult, op1=ALU.mult).then_inc(g_rdy, 1)

            def gated_low(h, i=0, per=0):
                dve.wait_ge(g_hi, lin(i, per, FT + h + 1))
                V.tensor_tensor(GL[:, h % 2, :], OB, GH[:, h % 2, :].bitcast(F32), ALU.subtract
                                ).then_inc(g_lo, 1)

            def block_of(h, i=0, per=0):
                prev, following = h > 0, per > 0 or h < HEADS - 1
                at, n0, pn = hg_tiles(prev, following), hg_start(h), per * HG_TILES
                sc = pieces(SC.rearrange("p c t -> p (c t)"))

                def pick(l):
                    n, mask = n0 + at[f"L{l}"], MASK[:, l:l + 1, :]
                    if l < STREAM_LEVELS:
                        V.copy_predicated(sc, mask.broadcast_to([P, NCH, CW]), ps(n)).then_inc(ps_free[n % 2], 1)
                    else:
                        V.copy_predicated(sc[:, 0:2, :], mask.broadcast_to([P, 2, CW]), ps_prompt(n)[0])
                        V.copy_predicated(sc[:, 2, 0:LAST_PROMPT], MASK[:, l, 0:LAST_PROMPT],
                                          ps_prompt(n)[1]).then_inc(ps_free[n % 2], 1)

                full(dve, n0 + at["L0"], i, pn)
                V.tensor_tensor(QF, QF, FG, ALU.mult).then_inc(kq, 1)
                pick(0)
                if prev:
                    diagonals(h - 1, i, per)
                for l in range(1, LEVELS):
                    if l > 1:
                        mine()
                    b = blocks(l - 1)[:, 0:tot[l][1], :]
                    a, w = tot[l]
                    dc.inc(V.tensor_tensor(TOT[:, a:a + w], b[:, :, 0], b[:, :, 1], ALU.mult))
                full(dve, n0 + at["V"], i, pn)
                scaled(n0 + at["V"], VK.rearrange("p c t -> p (c t)"))
                if prev:
                    gated(n0 + at["RB"], h - 1, i, per)

                def decayed(l):
                    full(dve, n0 + at[f"L{l}"], i, pn)
                    emptied(dve, n0 + at[f"L{l - 1}"], i, pn)
                    w, m = (T if l < STREAM_LEVELS else SEQ), 1 << (l - 1)
                    kr = KR[:, 0:w].rearrange("p (b h m) -> p b h m", h=2, m=m)
                    qf = QF[:, 0:w].rearrange("p (b h m) -> p b h m", h=2, m=m)
                    b = blocks(l - 1)[:, 0:w >> l, :]
                    if l == 1:
                        mine()
                    V.tensor_tensor(kr[:, :, 0, :], kr[:, :, 0, :],
                                    b[:, :, 1:2].broadcast_to([P, w >> l, m]), ALU.mult)
                    V.tensor_tensor(qf[:, :, 1, :], qf[:, :, 1, :],
                                    b[:, :, 0:1].broadcast_to([P, w >> l, m]), ALU.mult).then_inc(kq, 1)
                    pick(l)

                def adds(*ms):
                    for m in ms if prev else ():
                        add(n0 + at[f"W{m}"], m, None, i, pn)

                decayed(1)
                if prev:
                    gated_low(h - 1, i, per)
                full(dve, n0 + at["G"], i, pn)
                scaled(n0 + at["G"], GATE)
                decayed(2)
                adds(0)
                decayed(3)
                emptied(dve, n0 + at["VT"], i, pn)
                V.tensor_tensor(VM, VT[:, PCH:PCH + 1, :].broadcast_to([P, NB, P]),
                                ROWM.rearrange("p (b a) -> p b a", a=1).broadcast_to([P, NB, P]), ALU.mult
                                ).then_inc(vm_rdy, 1)
                if following:
                    full(dve, n0 + at["F"], i, pn)
                    scaled(n0 + at["F"], FG)
                decayed(4)
                adds(1, 2)
                decayed(5)
                adds(3, 4)
                decayed(6)
                adds(5, 6)
                decayed(7)
                adds(7)
                if following:
                    forget(h + 1, i, per)
                    full(dve, n0 + at["KT"], i, pn)
                    key()
                n = n0 + at["NS"]
                full(dve, n, i, pn)
                dve.wait_ge(state_in, lin(i, 16 * per, 16 * (h + 1)))
                a, w = tot[STREAM_LEVELS - 1]
                decay = TOT[:, a + w - NB:a + w].rearrange("p (b a) -> p b a", a=1)
                dc.inc(V.tensor_tensor(VM, SIN, decay.broadcast_to([P, NB, P]), ALU.mult))
                mine()
                V.tensor_tensor(VM[:, 0:6, :].rearrange("p (c b) v -> p c (b v)", c=2),
                                VM[:, 0:6, :].rearrange("p (c b) v -> p c (b v)", c=2), ps_prompt(n)[0], ALU.add)
                V.tensor_tensor(VM[:, 6:8, :].rearrange("p b v -> p (b v)"),
                                VM[:, 6:8, :].rearrange("p b v -> p (b v)"), ps_prompt(n)[1], ALU.add
                                ).then_inc(ps_free[n % 2], 1)
                full(dve, n0 + at["DS"], i, pn)
                a, w = tot[LEVELS - 1]
                for c in range(PCH):
                    new = ps_bank(n0 + at["DS"], c // 3)[:, (c % 3) * P:(c % 3 + 1) * P]
                    if c == 0:
                        ins = V.tensor_copy(ST[:, 0, :], new)
                    else:
                        mine()
                        ins = V.scalar_tensor_tensor(out=ST[:, c, :], in0=ST[:, c - 1, :],
                                                     scalar=TOT[:, a + c:a + c + 1], in1=new,
                                                     op0=ALU.mult, op1=ALU.add)
                    if c < PCH - 1:
                        dc.inc(ins)
                ins.then_inc(ps_free[(n0 + at["DS"]) % 2], 1)
                if following:
                    full(dve, n0 + at["O"], i, pn)
                    scaled(n0 + at["Q"], QF)

            full(dve, T_HG)
            scaled(T_HG, FG)
            forget(0)
            key()
            full(dve, T_HG + 1)
            scaled(T_HG + 1, QF)
            block_of(0)
            with dve.Fori(0, (HEADS - 2) // 2) as i:
                dc.enter(i, 2 * (1 + 7 + 7 + 1 + 1))
                for h in range(1, 3):
                    block_of(h, i, 2)
                dc.leave((HEADS - 2) // 2)
            block_of(HEADS - 1)
            diagonals(HEADS - 1)
            gated(T_F1 - KD - 1, HEADS - 1)
            gated_low(HEADS - 1)
            for m in range(KD):
                add(T_F1 - KD + m, m)
                if m:
                    low(P_F1, C_FFN1, m - 1)
            low(P_F1, C_FFN1, KD - 1)

            ffn(1, T_F1, M_F1, FT + HEADS, C_BD1, None)
            rstd(M_FIN)
            for m in range(KD):
                V.scalar_tensor_tensor(out=X[:, m, :], in0=X[:, m, :], scalar=PAR[:, C_FIN, m:m + 1],
                                       in1=RSTD[:], op0=ALU.mult, op1=ALU.mult).then_inc(y_rdy, 1)


def kernel(x_prompt, x_sample, cache_conv, state_hgrn, cache_ffn,
           norm_mix_w, norm_ffn_w, norm_final_w,
           cv_w_pw1, cv_b_pw1, cv_w_dw, cv_b_dw, cv_ln_g, cv_ln_b, cv_w_pw2, cv_b_pw2,
           hg_w_in, hg_lb_logits, hg_norm_w, hg_w_o,
           ff_w_up, ff_b_up, ff_w_dw, ff_b_dw, ff_w_down, ff_b_down):
    import numpy as np
    import concourse.bacc as bacc
    from concourse.bass_utils import run_bass_kernel_spmd as run

    def tiles(w):
        k, n = w.shape
        return w.reshape(k // P, P, n // P, P).transpose(2, 1, 0, 3)

    def units(w):
        return tiles(w).reshape(-1, P, 1024)

    def channels(v):
        return np.swapaxes(v.reshape(*v.shape[:-1], -1, P), -1, -2)

    arr = np.asarray
    pw1 = units(arr(cv_w_pw1)[0])
    stream = []
    for c in range(KD):
        stream += [pw1[KD + c], pw1[c]]
    stream += list(units(arr(cv_w_pw2)[0]))

    def ffn_units(layer):
        up = units(arr(ff_w_up)[layer])
        down = tiles(arr(ff_w_down)[layer])
        out = [up[0]]
        for j in range(FGROUPS):
            out += [up[FT + 2 * j], up[2 * j + 1], up[FT + 2 * j + 1]]
            if j < FGROUPS - 1:
                out.append(up[2 * j + 2])
            two = down[:, :, 2 * j:2 * j + 2, :]
            for half in range(2):
                out.append(two[4 * half:4 * half + 4].transpose(1, 0, 2, 3).reshape(P, 1024))
        return out

    stream += ffn_units(0)
    w_in, w_o = units(arr(hg_w_in)[0]), tiles(arr(hg_w_o)[0])
    of = [dict(zip("QFVG", (w_in[k * HEADS + h] for k in range(4))),
               W=w_o[:, :, h, :].transpose(1, 0, 2).reshape(P, 1024)) for h in range(HEADS)]
    stream += [of[0]["F"], of[0]["Q"]]
    for h in range(HEADS):
        stream += [of[h]["V"], of[h]["G"]] + ([of[h - 1]["W"]] if h else [])
        stream += [of[h + 1]["F"], of[h + 1]["Q"]] if h + 1 < HEADS else []
    stream.append(of[HEADS - 1]["W"])
    stream += ffn_units(1)
    assert len(stream) == UNITS

    x = np.concatenate([arr(x_prompt)[0], arr(x_sample).reshape(NB * NS, D)])
    x = x.T.reshape(KD, P, T)
    vecs = [arr(norm_mix_w)[0], arr(norm_mix_w)[1], arr(norm_ffn_w)[0], arr(norm_ffn_w)[1], arr(norm_final_w),
            arr(cv_b_pw1)[0, :D], arr(cv_b_pw1)[0, D:], arr(cv_b_dw)[0], arr(cv_ln_g)[0], arr(cv_ln_b)[0],
            arr(cv_b_pw2)[0], arr(ff_b_down)[0], arr(ff_b_down)[1], arr(hg_lb_logits)[0], arr(hg_norm_w)[0]]
    par = channels(np.stack(vecs)).transpose(1, 0, 2)
    taps = channels(arr(cv_w_dw)[0]).transpose(1, 0, 2)

    order = np.arange(2 * FT).reshape(2, FT).T.reshape(-1)
    ffp = np.stack([arr(ff_w_dw)[:, 0], arr(ff_w_dw)[:, 1], arr(ff_w_dw)[:, 2], arr(ff_b_up), arr(ff_b_dw)], 1)
    ffp = channels(ffp)[..., order].transpose(0, 2, 3, 1)
    fhist = channels(arr(cache_ffn).reshape(2, NB * 2, 2 * FF))[..., order].transpose(0, 2, 3, 1)
    chist = channels(arr(cache_conv)[0]).transpose(3, 2, 0, 1)
    state = arr(state_hgrn)[0].transpose(1, 2, 0, 3)

    s, t = np.arange(P)[:, None], np.arange(P)[None, :]
    const = np.concatenate([(s == t), np.ones((P, P), bool), (s // NS == np.arange(NB)[None, :])], 1)
    masks = [s == t]
    for l in range(1, LEVELS):
        m = 1 << (l - 1)
        masks.append((s // (2 * m) == t // (2 * m)) & (s % (2 * m) < m) & (t % (2 * m) >= m))
    mask = np.stack(masks, 1)

    nc = bacc.Bacc("TRN2", target_bir_lowering=False, num_devices=1)
    arrays, args = {}, []
    ins = {"w": np.stack(stream), "x": x, "par": par, "taps": taps, "ffp": ffp, "fhist": fhist, "chist": chist,
           "state": state, "const": const.astype(np.float32), "mask": mask.astype(np.float32)}
    for name, a in ins.items():
        a = np.ascontiguousarray(a)
        arrays["in_" + name] = a
        args.append(nc.dram_tensor("in_" + name, a.shape, mybir.dt.from_np(a.dtype), kind="ExternalInput").ap())
    outs = {"y": [KD, P, T], "convp": [P, KD, HIST], "convs": [KD, P, NB, HIST], "hgp": [HEADS, P, P],
            "hgs": [HEADS, P, NB, P], "ffn": [2, P, 2 * FT, 2 + 2 * NB]}
    for name, shape in outs.items():
        args.append(nc.dram_tensor("out_" + name, shape, F32, kind="ExternalOutput").ap())
    build(nc, *args)
    r = run(nc, [arrays], core_ids=[0]).results[0]

    y = r["out_y"].reshape(D, T).T
    convp = r["out_convp"].transpose(2, 1, 0).reshape(1, 1, HIST, D)
    convs = r["out_convs"].transpose(2, 3, 0, 1).reshape(1, NB, HIST, D)
    hgp = r["out_hgp"].reshape(1, 1, HEADS, P, P)
    hgs = r["out_hgs"].transpose(2, 0, 1, 3)[None]
    back = np.argsort(order)
    f = r["out_ffn"][:, :, back, :].transpose(0, 3, 2, 1).reshape(2, 2 + 2 * NB, 2 * FF)
    return (y[:SEQ][None], y[SEQ:].reshape(NB, NS, D), convp, hgp, f[:, None, 0:2], convs, hgs,
            f[:, 2:].reshape(2, NB, 2, 2 * FF))
```
